# Optimizing a Trainium2 kernel written in Bass

```python
import math
import jax, jax.numpy as jnp
from jax import lax
import numpy as np

D_MODEL = 1024
BATCH = 1
SEQ = 1024
DEPTH = 1
DEC_BATCH = 8
DEC_SEQ = 8
PAST_LEN = 2048
PAGE_SIZE = 128

N_HEADS = 8
HEAD_DIM = 64
N_KV_HEADS = 2
GROUP = N_HEADS // N_KV_HEADS
ATTN_WIDTH = N_HEADS * HEAD_DIM
KV_WIDTH = N_KV_HEADS * HEAD_DIM
WINDOW = 128
BLOCK = WINDOW
POOL_WIDTH = D_MODEL // 2
POOL_WINDOWS = (2, 4, 8, 16)
N_POOL_GROUPS = len(POOL_WINDOWS)
POOL_GROUP_WIDTH = POOL_WIDTH // N_POOL_GROUPS
POOL_STATE = max(POOL_WINDOWS) - 1
D_FF = 4 * D_MODEL
N_BUCKETS = 32
MAX_DISTANCE = 128
RMS_EPS = 1e-6
NEG_INF = -1e30
IN_WIDTH = ATTN_WIDTH + 2 * KV_WIDTH + POOL_WIDTH + 2 * D_MODEL
SPLITS = (ATTN_WIDTH, ATTN_WIDTH + KV_WIDTH, ATTN_WIDTH + 2 * KV_WIDTH,
          ATTN_WIDTH + 2 * KV_WIDTH + POOL_WIDTH,
          ATTN_WIDTH + 2 * KV_WIDTH + POOL_WIDTH + D_MODEL)

kernel_name = "hybrid_swa_sink_pool_gated_decode_step"

def rms_norm(x, g):
    xf = x.astype(jnp.float32)
    y = xf * lax.rsqrt(jnp.mean(xf * xf, axis=-1, keepdims=True) + RMS_EPS)
    return (y * g.astype(jnp.float32)).astype(x.dtype)

def rel_bucket(dist):
    d = jnp.maximum(dist, 0)
    max_exact = N_BUCKETS // 2
    large = max_exact + (jnp.log(jnp.maximum(d, 1).astype(jnp.float32) / max_exact)
                         / math.log(MAX_DISTANCE / max_exact)
                         * (N_BUCKETS - max_exact)).astype(jnp.int32)
    large = jnp.minimum(large, N_BUCKETS - 1)
    return jnp.where(d < max_exact, d, large)

def rel_bias(dist, table):
    b = table[rel_bucket(dist)]
    b = jnp.transpose(b, (2, 0, 1)).astype(jnp.float32)
    return b.reshape(N_KV_HEADS, GROUP, dist.shape[0], dist.shape[1])

def window_attention(q, k, v, valid, bias, sinks):
    s = jnp.einsum('bnqkgd,bnskd->bnkgqs', q, k,
                   preferred_element_type=jnp.float32) * (HEAD_DIM ** -0.5) + bias
    s = jnp.where(valid[None, :, None, None], s, NEG_INF)
    sink = sinks.astype(jnp.float32).reshape(1, 1, N_KV_HEADS, GROUP, 1, 1)
    m = jnp.maximum(jnp.max(s, axis=-1, keepdims=True), sink)
    p = jnp.exp(s - m)
    denom = jnp.sum(p, axis=-1, keepdims=True) + jnp.exp(sink - m)
    p = (p / denom).astype(v.dtype)
    return jnp.einsum('bnkgqs,bnskd->bnqkgd', p, v)

def pool_mix(ext, start_pos, w_grp, scale):
    B = ext.shape[0]
    T = ext.shape[1] - POOL_STATE
    cs = jnp.cumsum(jnp.pad(ext.astype(jnp.float32), ((0, 0), (1, 0), (0, 0))), axis=1)
    hi = cs[:, POOL_STATE + 1:]
    pos = start_pos + jnp.arange(T)
    parts = []
    for g, w in enumerate(POOL_WINDOWS):
        c = slice(g * POOL_GROUP_WIDTH, (g + 1) * POOL_GROUP_WIDTH)
        lo = cs[:, POOL_STATE + 1 - w:POOL_STATE + 1 - w + T, c]
        cnt = jnp.minimum(pos + 1, w).astype(jnp.float32)[None, :, None]
        parts.append((hi[..., c] - lo) / cnt)
    z = jnp.concatenate(parts, axis=-1) - ext[:, POOL_STATE:].astype(jnp.float32)
    z = z.astype(ext.dtype).reshape(B, T, N_POOL_GROUPS, POOL_GROUP_WIDTH)
    z = jnp.einsum('btgc,gcd->btgd', z, w_grp).reshape(B, T, POOL_WIDTH)
    return z * scale

def project_in(x, g_pre, w_in, b_in):
    u = rms_norm(x, g_pre) @ w_in + b_in
    return jnp.split(u, SPLITS, axis=-1)

def finish_layer(x, attn_o, pool_z, ga, gp, w_attn_up, w_pool_up, w_out,
                 g_post_mix, g_pre_mlp, g_post_mlp, w_mlp_up, w_mlp_down):
    a = attn_o @ w_attn_up
    p = pool_z @ w_pool_up
    m = jax.nn.sigmoid(ga) * a + jax.nn.sigmoid(gp) * p
    h = x + rms_norm(m @ w_out, g_post_mix)
    f = jnp.square(jax.nn.relu(rms_norm(h, g_pre_mlp) @ w_mlp_up)) @ w_mlp_down
    return h + rms_norm(f, g_post_mlp)

def setup_inputs(seed: int = 0) -> dict:
    key = jax.random.key(seed)
    ks = jax.random.split(key, 24)
    nrm = lambda k, shape, s: jax.random.normal(k, shape, jnp.float32) * s
    n_pages = PAST_LEN // PAGE_SIZE
    del n_pages
    return {
        "x_prompt": nrm(ks[0], (BATCH, SEQ, D_MODEL), 1.0),
        "x_sample": nrm(ks[1], (DEC_BATCH, DEC_SEQ, D_MODEL), 1.0),
        "cache_k_win": nrm(ks[2], (DEPTH, DEC_BATCH, WINDOW, N_KV_HEADS, HEAD_DIM), 1.0),
        "cache_v_win": nrm(ks[3], (DEPTH, DEC_BATCH, WINDOW, N_KV_HEADS, HEAD_DIM), 1.0),
        "state_pool": nrm(ks[4], (DEPTH, DEC_BATCH, POOL_STATE, POOL_WIDTH), 1.0),
        "norm_pre_mix": 1.0 + nrm(ks[5], (DEPTH, D_MODEL), 0.05),
        "norm_post_mix": 1.0 + nrm(ks[6], (DEPTH, D_MODEL), 0.05),
        "norm_pre_mlp": 1.0 + nrm(ks[7], (DEPTH, D_MODEL), 0.05),
        "norm_post_mlp": 1.0 + nrm(ks[8], (DEPTH, D_MODEL), 0.05),
        "w_in": nrm(ks[9], (DEPTH, D_MODEL, IN_WIDTH), D_MODEL ** -0.5),
        "b_in": nrm(ks[10], (DEPTH, IN_WIDTH), 0.02),
        "attn_sinks": nrm(ks[11], (DEPTH, N_HEADS), 0.5),
        "rel_bias_table": nrm(ks[12], (N_BUCKETS, N_HEADS), 0.5),
        "w_attn_up": nrm(ks[13], (DEPTH, ATTN_WIDTH, D_MODEL), ATTN_WIDTH ** -0.5),
        "w_pool_grp": nrm(ks[14], (DEPTH, N_POOL_GROUPS, POOL_GROUP_WIDTH, POOL_GROUP_WIDTH), POOL_GROUP_WIDTH ** -0.5),
        "pool_scale": 1.0 + nrm(ks[15], (DEPTH, POOL_WIDTH), 0.1),
        "w_pool_up": nrm(ks[16], (DEPTH, POOL_WIDTH, D_MODEL), POOL_WIDTH ** -0.5),
        "w_out": nrm(ks[17], (DEPTH, D_MODEL, D_MODEL), D_MODEL ** -0.5),
        "w_mlp_up": nrm(ks[18], (DEPTH, D_MODEL, D_FF), D_MODEL ** -0.5),
        "w_mlp_down": nrm(ks[19], (DEPTH, D_FF, D_MODEL), D_FF ** -0.5),
    }

def reference(x_prompt, x_sample, cache_k_win, cache_v_win, state_pool,
              norm_pre_mix, norm_post_mix, norm_pre_mlp, norm_post_mlp,
              w_in, b_in, attn_sinks, rel_bias_table, w_attn_up, w_pool_grp,
              pool_scale, w_pool_up, w_out, w_mlp_up, w_mlp_down):
    B, S, _ = x_prompt.shape
    NB = S // BLOCK
    DB, T, _ = x_sample.shape

    r = jnp.arange(BLOCK)[:, None]
    j = jnp.arange(2 * BLOCK)[None, :]
    dist_p = r + BLOCK - j
    key_pos_p = jnp.arange(NB)[:, None, None] * BLOCK - BLOCK + j[None]
    valid_p = (dist_p >= 0)[None] & (dist_p < WINDOW)[None] & (key_pos_p >= 0)
    bias_p = rel_bias(dist_p, rel_bias_table)

    i_s = jnp.arange(T)[:, None]
    j_s = jnp.arange(WINDOW + T)[None, :]
    dist_s = i_s + WINDOW - j_s
    valid_s = ((dist_s >= 0) & (dist_s < WINDOW) & (PAST_LEN - WINDOW + j_s >= 0))[None]
    bias_s = rel_bias(dist_s, rel_bias_table)

    def band(t):
        tp = jnp.pad(t, ((0, 0), (BLOCK, 0), (0, 0), (0, 0)))
        tp = tp.reshape(B, NB + 1, BLOCK, N_KV_HEADS, HEAD_DIM)
        return jnp.concatenate([tp[:, :-1], tp[:, 1:]], axis=2)

    hp, hs = x_prompt, x_sample
    kp_l, vp_l, pp_l, ks_l, vs_l, ps_l = [], [], [], [], [], []
    for l in range(DEPTH):
        tail = (w_attn_up[l], w_pool_up[l], w_out[l], norm_post_mix[l],
                norm_pre_mlp[l], norm_post_mlp[l], w_mlp_up[l], w_mlp_down[l])

        q, k, v, up, ga, gp = project_in(hp, norm_pre_mix[l], w_in[l], b_in[l])
        q = q.reshape(B, NB, BLOCK, N_KV_HEADS, GROUP, HEAD_DIM)
        k = k.reshape(B, S, N_KV_HEADS, HEAD_DIM)
        v = v.reshape(B, S, N_KV_HEADS, HEAD_DIM)
        o = window_attention(q, band(k), band(v), valid_p, bias_p, attn_sinks[l])
        o = o.reshape(B, S, ATTN_WIDTH)
        ext = jnp.pad(up, ((0, 0), (POOL_STATE, 0), (0, 0)))
        z = pool_mix(ext, 0, w_pool_grp[l], pool_scale[l])
        kp_l.append(k[:, -WINDOW:])
        vp_l.append(v[:, -WINDOW:])
        pp_l.append(up[:, -POOL_STATE:])
        hp = finish_layer(hp, o, z, ga, gp, *tail)

        q, k, v, up, ga, gp = project_in(hs, norm_pre_mix[l], w_in[l], b_in[l])
        q = q.reshape(DB, 1, T, N_KV_HEADS, GROUP, HEAD_DIM)
        kx = jnp.concatenate([cache_k_win[l], k.reshape(DB, T, N_KV_HEADS, HEAD_DIM)], axis=1)
        vx = jnp.concatenate([cache_v_win[l], v.reshape(DB, T, N_KV_HEADS, HEAD_DIM)], axis=1)
        o = window_attention(q, kx[:, None], vx[:, None], valid_s, bias_s, attn_sinks[l])
        o = o.reshape(DB, T, ATTN_WIDTH)
        ext = jnp.concatenate([state_pool[l], up], axis=1)
        z = pool_mix(ext, PAST_LEN, w_pool_grp[l], pool_scale[l])
        ks_l.append(kx[:, -WINDOW:])
        vs_l.append(vx[:, -WINDOW:])
        ps_l.append(ext[:, -POOL_STATE:])
        hs = finish_layer(hs, o, z, ga, gp, *tail)

    return (hp, hs, jnp.stack(kp_l), jnp.stack(vp_l), jnp.stack(pp_l),
            jnp.stack(ks_l), jnp.stack(vs_l), jnp.stack(ps_l))


_drawn_inputs = setup_inputs


def setup_inputs(seed=0):
    import zlib

    import numpy as np

    out = dict(_drawn_inputs(seed))
    spreads = {}
    factors = {'b_in': 2.69, 'attn_sinks': 8.0}
    for name, (base, spread) in spreads.items():
        noise = np.random.default_rng([zlib.crc32(name.encode()), seed]).standard_normal(out[name].shape)
        drawn = base * np.exp(spread * noise) if base else spread * noise
        out[name] = __import__('jax').numpy.asarray(drawn.astype(out[name].dtype))
    for name, factor in factors.items():
        out[name] = (out[name] * factor).astype(out[name].dtype)
    return out
```

```python
import math
from contextlib import ExitStack

import numpy as np
import concourse.bass as bass
from concourse import mybir

D = 1024
SEQ = 1024
NB_DEC, T_DEC = 8, 8
SROWS = NB_DEC * T_DEC
ROWS = SEQ + SROWS
P = 128
KD = D // P
HEADS, HD, KVH = 8, 64, 2
GRP = HEADS // KVH
KVW = KVH * HD
AW = HEADS * HD
WIN = 128
PW = D // 2
PT_ = PW // P
PSTATE = 15
DFF = 4 * D
BUCKETS, MAXD = 32, 128
EPS = 1e-6
NEG = -1e30
IN_W = AW + 2 * KVW + PW + 2 * D
COL_K, COL_V, COL_UP = AW, AW + KVW, AW + 2 * KVW
COL_GA, COL_GP = COL_UP + PW, COL_UP + PW + D
CH = [(0, 384), (384, 384), (768, ROWS - 768)]
NC_ = len(CH)
NBLK = SEQ // P
RT = NBLK + 1
KXW = WIN + T_DEC
FB = 4
NFB = DFF // (FB * P)
FY = 3 * P
SCALE = HD ** -0.5

U_K, U_V, U_Q, U_UP = 0, 1, 2, 6
U_D = 10
U_E = U_D + 3 * KD
U_M = U_E + KD
N_UNITS = U_M + 8 * NFB

G_GRP = 3 * U_D
G_D = G_GRP + 3 * PT_
G_E = G_D + 12 * KD
G_M = G_E + 3 * KD
UP_G, DOWN_G = 3 * FB, 3 * KD
N_GROUPS = G_M + (UP_G + DOWN_G) * NFB
LAST = NFB - 1


def group_reader(g):
    if g < G_GRP:
        unit = g // 3
        return "A" if unit == U_V or unit >= U_UP else "D"
    if g < G_D:
        return "D"
    if g < G_E:
        return "A" if (g - G_D) % 12 < 6 else "D"
    if g < G_M:
        return "D"
    return "A" if (g - G_M) % (UP_G + DOWN_G) < UP_G else "D"


FREED = []
_n = {"A": 0, "D": 0}
for _g in range(N_GROUPS):
    _e = group_reader(_g)
    _n[_e] += 1
    FREED.append((_e, _n[_e]))


def raw_dmas(n):
    if U_Q <= n < U_UP:
        return 2
    if U_D <= n < U_E and (n - U_D) % 3 == 2:
        return 3
    return 1


def unit_end(n):
    if n < U_D:
        return 3 * n + 3
    if n < U_E:
        j, x = divmod(n - U_D, 3)
        return G_D + 12 * j + (3, 6, 12)[x]
    if n < U_M:
        return G_E + 2 * KD + (n - U_E) + 1
    blk, x = divmod(n - U_M, 8)
    base = G_M + (UP_G + DOWN_G) * blk
    if x < FB:
        return base + (2 * FB + x + 1 if blk == 0 else 3 * x + 3)
    v = x - FB
    return base + UP_G + (2 * KD + 2 * v + 2 if blk == LAST else 6 * v + 6)


RAW = []
_s = [0, 0]
for _u in range(N_UNITS):
    _s[_u % 2] += 16 * raw_dmas(_u)
    RAW.append(_s[_u % 2])


def per_block(value_of, blk):
    if isinstance(blk, int):
        return value_of(blk)
    v1, v2 = value_of(1), value_of(2)
    return blk * (v2 - v1) + (2 * v1 - v2)


A_UNITS = 2 * NBLK + 1
A_STEPS = A_UNITS + 4
FILL = [0, 1, 3, 4, 6, 7, 9, 10, 12, 13, 15, 16]
POOL_PIECES = [(640, 384), (256, 384), (0, 256)]


def build(nc, I, O):
    f32, f32r = mybir.dt.float32, mybir.dt.float32r
    ALU, ACT = mybir.AluOpType, mybir.ActivationFunctionType
    ctx = ExitStack()
    with ctx:
        T = ROWS * 4

        def at(name, shape, off, dt=f32):
            return nc.alloc_sbuf_tensor_at(name, shape, dt, offset=16512 + off)

        XN, R16, R24, R32 = 0, 16 * T, 24 * T, 32 * T
        A1 = R16 + 19584
        A2 = R32 + 18432
        A3 = 40 * T
        CON = A3 + 8704
        RING = CON + 5472

        xn = at("xn", [P, 2, KD, ROWS], XN, f32r)
        xrow = at("xrow", [P, NBLK, D], R24)
        xrow_s = at("xrow_s", [SROWS, D], A2 + 5120)
        gbc = at("gbc", [P, D], A2 + 9216)
        xsq = at("xsq", [P, D], A2)
        anti = at("anti", [P, P], A2 + 4096)
        rs = at("rs", [P, RT], A2 + 4608)
        ss = at("ss", [P, RT], RING - 64)
        bias_rev = at("bias_rev", [P, HEADS, 2 * WIN], R16)
        kcache = at("kcache", [P, NB_DEC, KVW], R16 + 8192)
        state_in = at("state_in", [NB_DEC * PSTATE, PW], R16 + 12288)
        brow = at("brow", [HEADS, FY], R16 + 14336)
        onehot = at("onehot", [BUCKETS, P], R16 + 15872)
        table = at("table", [BUCKETS, HEADS], R16 + 16384)
        upp = at("upp", [P, PT_, PSTATE + SEQ], R16)
        ups = at("ups", [P, PT_, NB_DEC, PSTATE + T_DEC], R16 + 16640)
        bias = at("bias", [P, HEADS, 2 * WIN], A1)
        orow = at("orow", [P, GRP, KVH, HD], A1 + 8192)
        wgrp = at("wgrp", [P, PT_, P], A1 + 10240)
        bias_s = at("bias_s", [P, KVH, KXW + 1], A1 + 12288)
        stat = at("stat", [P, 7, 4, 4], A1 + 13408)
        tails = at("tails", [P, PT_, PSTATE + SROWS], A1 + 13856)
        qo = at("qo", [P, 2, GRP, ROWS], R24, f32r)
        kk = at("kk", [P, 2, ROWS], R32, f32r)
        vT = at("vT", [P, ROWS], R32 + 2 * T)
        vnew = at("vnew", [T_DEC, NB_DEC, KVW], R32 + 2 * T)
        vr = at("vr", [P, NBLK, KVW], R32 + 3 * T)
        kf = at("kf", [P, WIN + SROWS], R32 + 3 * T + 4096)
        pr = at("pr", [P, 2, 4, 2 * WIN], A2)
        pt = at("pt", [P, 8, P], A2 + 8192)
        pool_s = [at(f"pool_s{i}", [P, 399], A2 + 12288 + 1600 * i) for i in range(2)]
        inv_cnt = at("inv_cnt", [P, PT_, 16], A2 + 15488)
        kxT = at("kxT", [P, NB_DEC, KXW], A3)
        qs = at("qs", [P, NB_DEC, GRP, T_DEC], A3 + 4352)
        src_s = at("src_s", [32, KVH, KXW + 1], A3 + 5376)
        perm_s = at("perm_s", [32, P], A3 + 6496)
        vecrow = at("vecrow", [62, P], A3 + 7008)
        kout = at("kout", [P, 2, KVW], A3 + 7520)
        vcache = at("vcache", [P, NB_DEC, KVW], CON + 1312)
        stout = at("stout", [P, 2, PW], CON + 1312)
        zz = at("zz", [P, 2, PT_, ROWS], R32, f32r)
        sga = at("sga", [P, ROWS], A3)
        sgp = at("sgp", [P, ROWS], A3 + T)
        mix = at("mix", [P, KD, ROWS], R16)
        hh = at("hh", [P, KD, ROWS], R16)
        wo = at("wo", [P, KD, 2, D], R24, f32r)
        xre = at("xre", [P, KD, ROWS], XN)
        xre_s = at("xre_s", [SROWS, KD, P], R24 + KD * 2 * D * 4)
        sqa = [at(f"sqa{i}", [P, 384], A3 + 1536 * i) for i in range(2)]
        ssa = at("ssa", [P, 384], A3 + 3072)
        rstd = at("rstd", [P, 384], A3 + 4608)
        sqb = [at("sqb0", [P, 384], A3 + 6144), at("sqb1", [P, 384], CON + 1312)]
        ssb = at("ssb", [P, 384], CON + 2848)
        acc = at("acc", [P, KD, ROWS], R24)
        ff = at("ff", [P, 2, FB, ROWS], R32, f32r)
        xw = at("xw", [P, 2, 2, D], XN, f32r)
        yrow = at("yrow", [P, RT, D], XN + 16384)
        ident = at("ident", [P, P], CON)
        ones = at("ones", [P, P], CON + 512)
        vec = at("vec", [P, 64], CON + 1024)
        sink = at("sink", [P, HEADS], CON + 1280)
        V_G1, V_G2, V_G3, V_PS, V_EPS = 34, 42, 50, 58, 62
        eps = vec[:, V_EPS:V_EPS + 1]
        raw = at("raw", [P, 2, D], RING)
        wr = at("wr", [P, 2, 2, D], RING + 8192, f32r)

        ps = ctx.enter_context(nc.psum_tensor("ps", [P, 8, 512], f32))
        bias_dram = nc.dram_tensor("bias_by_distance", [HEADS, FY], f32).ap()

        def sem(name):
            return ctx.enter_context(nc.semaphore(name))

        raw_in = [sem(f"raw_in{i}") for i in range(2)]
        w_hi, w_lo, done = sem("w_hi"), sem("w_lo"), sem("group_done")
        freed = {"A": sem("freed_by_scalar"), "D": sem("freed_by_vector")}
        x_in = [sem(f"x_in{i}") for i in range(RT)]
        gbc_in, vec_in, tab_in, kc_in, st_in = (sem(n) for n in ("gbc_in", "vec_in", "tab_in", "kc_in", "st_in"))
        late_in, src_in, rev_in, brow_out = (sem(n) for n in ("late_in", "src_in", "rev_in", "brow_out"))
        zeroed, consts = sem("zeroed"), sem("consts")
        x_ss, x_sd, x_rs, x_n, x_t, x_hi, x_lo = (sem("x_" + n) for n in ("ss", "sd", "rs", "n", "t", "hi", "lo"))
        vec_t, vec_r, brow_p, brow_r = (sem(n) for n in ("vec_t", "vec_r", "brow_p", "brow_r"))
        kc_t, kc_r, st_t, st_r = (sem(n) for n in ("kc_t", "kc_r", "st_t", "st_r"))
        sb_p, sb_r, bias_p, bias_r, pads = (sem(n) for n in ("sb_p", "sb_r", "bias_p", "bias_r", "pads"))
        v_t, v_r, vn_r, ko_r, kf_r, in_hi = (sem(n) for n in ("v_t", "v_r", "vn_r", "ko_r", "kf_r", "in_hi"))
        qk, s_free, stats, dvs, expd = (sem(n) for n in ("qk", "s_free", "stats", "dvs", "expd"))
        pt_t, pt_a, pt_d, pv = (sem(n) for n in ("pt_t", "pt_a", "pt_d", "pv"))
        o_norm, o_t, o_hi, o_lo = (sem(n) for n in ("o_norm", "o_t", "o_hi", "o_lo"))
        pl, pooled, st_o, st_or, z_hi = (sem(n) for n in ("pool_steps", "pooled", "st_o", "st_or", "z_hi"))
        mixed, m_hi, m_lo, e_sq, e_add = (sem(n) for n in ("mixed", "m_hi", "m_lo", "e_sq", "e_add"))
        n_sum, n_sd, n_rs, n_t, n_h, n_sq, n_add = (sem("n_" + n) for n in ("sum", "sd", "rs", "t", "h", "sq", "add"))
        n2_t, n2_hi, n2_lo, xr_in, xr_t = (sem(n) for n in ("n2_t", "n2_hi", "n2_lo", "xr_in", "xr_t"))
        f_sq, f_hi, f_lo = sem("f_sq"), sem("f_hi"), sem("f_lo")
        y_t, y_h, y_p, y_ra, y_rd = (sem(n) for n in ("y_t", "y_h", "y_p", "y_ra", "y_rd"))
        y_out, moved_out, rows_out, state_out = (sem(n) for n in ("y_out", "moved_out", "rows_out", "state_out"))
        block = ctx.enter_context(nc.Block())

        def bank_of(g):
            return g % 2 if g < G_GRP else g % 4

        def before_in_bank(g):
            q = g - 1
            while q >= 0 and bank_of(q) != bank_of(g):
                q -= 1
            return q

        def slot(n):
            if U_E <= n < U_M:
                s, i = wo, n - U_E
            elif U_M <= n < U_M + FB:
                s, i = wo, n - U_M
            elif n >= N_UNITS - 2:
                s, i = xw, n % 2
            else:
                s, i = wr, n % 2
            return s[:, i, 0, :], s[:, i, 1, :]

        def slot_free(n):
            if U_E <= n < U_M:
                return G_E
            if U_M <= n < U_M + FB:
                return unit_end(U_E + n - U_M)
            if n in (U_M + FB, U_M + FB + 1):
                return G_E
            if n >= N_UNITS - 2:
                return unit_end(N_UNITS - 5)
            return unit_end(n - 2) if n >= 2 else 0

        def is_block(blk, n):
            return isinstance(blk, int) and blk == n

        def g_up(blk, j, c):
            return G_M + (UP_G + DOWN_G) * blk + (FB * c + j if is_block(blk, 0) else NC_ * j + c)

        def g_down(blk, m, c):
            return G_M + (UP_G + DOWN_G) * blk + UP_G + (KD * c + m if is_block(blk, LAST) else NC_ * m + c)

        def e_up(blk, j, c):
            return UP_G * blk + (FB * c + j if is_block(blk, 0) else NC_ * j + c)

        def cs(c):
            return slice(CH[c][0], CH[c][0] + CH[c][1])

        MAIN = [(j, c) for j in range(FB) for c in range(NC_)]
        DOWN = [(m, c) for m in range(KD) for c in range(NC_)]
        U_LASTD = U_M + 8 * LAST + FB
        STAGE3 = [(j, c) for c in range(2) for j in range(FB)]

        def bank_up(blk, j, c):
            return bank_of(g_up(blk if isinstance(blk, int) else 1, j, c))

        def bank_down(blk, m, c):
            return bank_of(g_down(blk if isinstance(blk, int) else 1, m, c))

        def vcol(n):
            return {U_K: GRP, U_V: GRP + 1}.get(n, n - U_Q if n < U_UP else n)

        MX, MM, NM, DD, ES, LL, RR = range(7)

        def keys(u):
            return (WIN, WIN) if u < 2 else (0, 2 * WIN) if u < A_UNITS - 1 else (0, KXW)

        def scores(i):
            return ps[:, 2 + i // 2, (i % 2) * 2 * WIN:(i % 2 + 1) * 2 * WIN]

        def sample_out(part, half):
            c0 = SEQ + half * 4 * T_DEC
            dst = qo[:, part, :, c0:c0 + 4 * T_DEC].rearrange("p i (b t) -> p i b t", t=T_DEC)
            src = ps[:, 7, half * P:(half + 1) * P].rearrange("p (b i t) -> p i b t", b=4, i=GRP)
            return dst, src

        @block.sync
        def _(sp):
            w_in, wau, wpu = I["w_in"][0], I["w_attn_up"][0], I["w_pool_up"][0]
            w_up = I["w_mlp_up"][0].rearrange("(k p) (b j n) -> b j p k n", p=P, b=NFB, j=FB)
            w_dn = I["w_mlp_down"][0].rearrange("(b k p) (v n) -> b v p k n", p=P, b=NFB, v=4)

            def cols(w, c0, n=P):
                return w[:, c0:c0 + n].rearrange("(k p) n -> p k n", p=P)

            def tiles(n):
                return raw[:, n % 2, :].rearrange("p (k n) -> p k n", n=P)

            def load(n, pieces):
                if n >= 2:
                    sp.wait_ge(w_lo, n - 1)
                for dst, src in pieces:
                    sp.dma_start(dst, src).then_inc(raw_in[n % 2], 16)

            for r in range(RT):
                if r < NBLK:
                    sp.dma_start(xrow[:, r, :], I["x_prompt"][0, r * P:(r + 1) * P, :]).then_inc(x_in[r], 16)
                else:
                    sp.dma_start(xrow_s[:, :], I["x_sample"].rearrange("b t n -> (b t) n")).then_inc(x_in[r], 16)
                if r == 2:
                    load(U_K, [(tiles(U_K), cols(w_in, COL_K))])
                if r == 4:
                    load(U_V, [(tiles(U_V), cols(w_in, COL_V))])
            for i in range(GRP):
                load(U_Q + i, [(tiles(U_Q + i)[:, :, g * HD:(g + 1) * HD], cols(w_in, (g * GRP + i) * HD, HD))
                               for g in range(KVH)])
            for t in range(PT_):
                load(U_UP + t, [(tiles(U_UP + t), cols(w_in, COL_UP + t * P))])
            for j in range(KD):
                n = U_D + 3 * j
                load(n, [(tiles(n), cols(w_in, COL_GA + j * P))])
                load(n + 1, [(tiles(n + 1), cols(w_in, COL_GP + j * P))])
                au = wau[:, j * P:(j + 1) * P].rearrange("(g i d) n -> g d i n", g=KVH, i=GRP)
                load(n + 2, [(tiles(n + 2)[g * HD:(g + 1) * HD, 0:GRP, :], au[g]) for g in range(KVH)]
                     + [(tiles(n + 2)[:, GRP:KD, :], cols(wpu, j * P))])
            for e in range(KD):
                load(U_E + e, [(tiles(U_E + e), cols(I["w_out"][0], e * P))])
            with sp.Fori(0, NFB) as blk:
                for x in range(8):
                    sp.wait_ge(w_lo, blk * 8 + (U_M + x - 1))
                    if x < FB:
                        sp.dma_start(tiles(x), w_up[blk, x]).then_inc(raw_in[x % 2], 16)
                    else:
                        sp.dma_start(raw[:, x % 2, :].rearrange("p (k n) -> p k n", k=FB), w_dn[blk, x - FB])\
                            .then_inc(raw_in[x % 2], 16)
            for r in range(RT):
                sp.wait_ge(y_ra, r + 1)
                sp.wait_ge(y_rd, r + 1)
                if r < NBLK:
                    sp.dma_start(O["y_prompt"][0, r * P:(r + 1) * P, :], yrow[:, r, :]).then_inc(y_out, 16)
                else:
                    sp.dma_start(O["y_sample"].rearrange("b t n -> (b t) n"), yrow[0:SROWS, r, :]).then_inc(y_out, 16)
            sp.wait_ge(y_out, 16 * RT)

        @block.gpsimd
        def _(pool):
            pool.memset(ident[:, :], 0.0).then_inc(zeroed, 1)
            pool.memset(anti[:, :], 0.0).then_inc(zeroed, 1)
            pool.memset(brow[:, :], NEG).then_inc(consts, 1)
            pool.memset(ones[:, :], 1.0).then_inc(consts, 1)
            pool.memset(eps, EPS).then_inc(consts, 1)
            pool.wait_ge(zeroed, 2)
            pool.affine_select(out=ident[:, :], in_=ident[:, :], compare_op=ALU.not_equal, fill=1.0,
                               base=0, pattern=[[-1, P]], channel_multiplier=1).then_inc(consts, 1)
            pool.affine_select(out=anti[:, :], in_=anti[:, :], compare_op=ALU.not_equal, fill=1.0,
                               base=1 - P, pattern=[[1, P]], channel_multiplier=1).then_inc(consts, 1)
            pool.dma_start(gbc[:, :], I["norm_pre_mix"].to_broadcast([P, D])).then_inc(gbc_in, 16)
            pool.dma_start(table[:, :], I["rel_bias_table"]).then_inc(tab_in, 16)
            pool.dma_start(onehot[:, :], I["bucket_onehot"]).then_inc(tab_in, 16)
            b = I["b_in"][0]
            for g in range(KVH):
                pool.dma_start(vecrow[0:GRP, g * HD:(g + 1) * HD],
                               b[g * GRP * HD:(g + 1) * GRP * HD].rearrange("(i d) -> i d", d=HD)).then_inc(vec_in, 16)
            pool.dma_start(vecrow[GRP:26, :], b[AW:IN_W].rearrange("(t p) -> t p", p=P)).then_inc(vec_in, 16)
            for i, name in enumerate(("norm_pre_mix", "norm_post_mix", "norm_pre_mlp", "norm_post_mlp")):
                pool.dma_start(vecrow[26 + KD * i:26 + KD * (i + 1), :], I[name][0].rearrange("(t p) -> t p", p=P))\
                    .then_inc(vec_in, 16)
            pool.dma_start(vecrow[58:62, :], I["pool_scale"][0].rearrange("(t p) -> t p", p=P)).then_inc(vec_in, 16)
            pool.dma_start(kcache[:, :, :], I["cache_k_win"][0].rearrange("b s g d -> s b (g d)")).then_inc(kc_in, 16)
            pool.dma_start(state_in[:, :], I["state_pool"][0].rearrange("b s n -> (b s) n")).then_inc(st_in, 16)
            pool.wait_ge(brow_r, 1)
            pool.dma_start(bias_dram, brow[:, :]).then_inc(brow_out, 16)
            pool.wait_ge(brow_out, 16)
            pool.dma_start(bias_rev[:, :, :], bass.AP(tensor=bias_dram.tensor, offset=0,
                           ap=[[1, P], [FY, HEADS], [1, 2 * WIN]])).then_inc(rev_in, 16)
            for i in range(GRP):
                pool.dma_start(src_s[T_DEC * i:T_DEC * (i + 1), :, 0:KXW], bass.AP(
                    tensor=bias_dram.tensor, offset=FY * i + WIN - T_DEC,
                    ap=[[1, T_DEC], [FY * GRP, KVH], [1, KXW]])).then_inc(src_in, 16)
                pool.dma_start(src_s[T_DEC * i:T_DEC * (i + 1), :, KXW:KXW + 1], bass.AP(
                    tensor=I["attn_sinks"].tensor, offset=i,
                    ap=[[0, T_DEC], [GRP, KVH], [1, 1]]), allow_slow_non_contiguous=True).then_inc(src_in, 16)
            pool.dma_start(perm_s[:, :], I["query_perm"]).then_inc(src_in, 16)
            pool.dma_start(sink[:, :], I["attn_sinks"].to_broadcast([P, HEADS])).then_inc(src_in, 16)
            pool.dma_start(vcache[:, :, :], I["cache_v_win"][0].rearrange("b s g d -> s b (g d)")).then_inc(late_in, 16)
            pool.dma_start(wgrp[:, :, :], I["w_pool_grp"][0].rearrange("t c d -> c t d")).then_inc(late_in, 16)
            pool.dma_start(inv_cnt[:, :, :].rearrange("p t n -> p (t n)"),
                           I["inv_count"].to_broadcast([P, PT_ * 16])).then_inc(late_in, 16)
            for src, dst in (("cache_k_win", "k_win_sample"), ("cache_v_win", "v_win_sample")):
                pool.dma_start(O[dst][0, :, 0:WIN - T_DEC].rearrange("b s g d -> b (s g d)"),
                               I[src][0, :, T_DEC:WIN].rearrange("b s g d -> b (s g d)")).then_inc(moved_out, 16)
            pool.dma_start(O["pool_state_sample"][0, :, 0:PSTATE - T_DEC].rearrange("b s n -> b (s n)"),
                           I["state_pool"][0, :, T_DEC:PSTATE].rearrange("b s n -> b (s n)")).then_inc(moved_out, 16)
            pool.wait_ge(bias_p, 1)
            pool.wait_ge(kc_t, 1)
            pool.wait_ge(st_t, 1)
            pool.memset(upp[:, :, 0:PSTATE], 0.0).then_inc(pads, 1)
            pool.wait_ge(ko_r, 2)
            pool.dma_start(O["k_win_prompt"][0, 0].rearrange("s g d -> s (g d)"), kout[:, 0, :]).then_inc(rows_out, 16)
            pool.dma_start(O["k_win_sample"][0, :, WIN - T_DEC:WIN].rearrange("b t g d -> b t (g d)"),
                           kout[0:SROWS, 1, :]).then_inc(rows_out, 16)
            pool.wait_ge(v_r, 1)
            pool.dma_start(O["v_win_prompt"][0, 0].rearrange("s g d -> s (g d)"), vr[:, NBLK - 1, :]).then_inc(rows_out, 16)
            pool.wait_ge(vn_r, 1)
            pool.dma_start(O["v_win_sample"][0, :, WIN - T_DEC:WIN].rearrange("b t g d -> t b (g d)"),
                           vnew[:, :, :]).then_inc(rows_out, 16)

            steps = [0]

            def chained(ins):
                steps[0] += 1
                ins.then_inc(pl, 1)
                pool.wait_ge(pl, steps[0])

            def window(src, scratch, w, width, at_col):
                span, cur, n, i = 1, src, width + w - 1, 0
                base = at_col - (w - 1)
                while span < w:
                    n -= span
                    chained(pool.tensor_tensor(scratch[i % 2](0, n), cur(base + span, n), cur(base, n), ALU.add))
                    cur, base, span, i = scratch[i % 2], 0, 2 * span, i + 1
                return cur

            pool.wait_ge(late_in, 16 * 3)
            pool.wait_ge(pads, 1)
            EXT = PSTATE + T_DEC
            row = [lambda a, n, q=pool_s[i]: q[:, a:a + n] for i in range(2)]
            per_seq = [lambda a, n, q=pool_s[i]: q[:, 0:NB_DEC * EXT].rearrange("p (b s) -> p b s", s=EXT)[:, :, a:a + n]
                       for i in range(2)]
            for t in range(PT_):
                w = 2 ** (t + 1)
                pool.wait_ge(freed["A"], FREED[3 * (U_UP + t) + 2][1])
                chained(pool.tensor_copy(tails[:, t, 0:PSTATE], upp[:, t, SEQ:SEQ + PSTATE]))
                chained(pool.tensor_copy(tails[:, t, PSTATE:].rearrange("p (b s) -> p b s", s=T_DEC),
                                         ups[:, t, :, PSTATE:]))
                for c0, width in POOL_PIECES:
                    s = window(lambda a, n: upp[:, t, a:a + n], row, w, width, PSTATE + c0)
                    x = upp[:, t, PSTATE + c0:PSTATE + c0 + width]
                    first = 16 if c0 == 0 else 0
                    if first:
                        chained(pool.tensor_tensor(s(0, first), s(0, first), inv_cnt[:, t, :], ALU.mult))
                    chained(pool.tensor_scalar(s(first, width - first), s(first, width - first), 1.0 / w, None, ALU.mult))
                    chained(pool.tensor_tensor(x, s(0, width), x, ALU.subtract))
                s = window(lambda a, n: ups[:, t, :, a:a + n], per_seq, w, T_DEC, PSTATE)
                chained(pool.tensor_scalar(s(0, T_DEC), s(0, T_DEC), 1.0 / w, None, ALU.mult))
                x = ups[:, t, :, PSTATE:]
                steps[0] += 1
                pool.tensor_tensor(x, s(0, T_DEC), x, ALU.subtract).then_inc(pl, 1)
                pool.wait_ge(pl, steps[0])
                pool.sem_inc(pooled, 1)
            pool.wait_ge(st_or, 2)
            pool.dma_start(O["pool_state_prompt"][0, 0], stout[0:PSTATE, 0, :]).then_inc(state_out, 16)
            pool.dma_start(O["pool_state_sample"][0, :, PSTATE - T_DEC:PSTATE].rearrange("b t n -> b t n"),
                           stout[0:SROWS, 1, :]).then_inc(state_out, 16)

            def add_product_squares(c, m):
                if m:
                    pool.wait_ge(e_sq, KD * c + m + 1)
                    if m > 1:
                        pool.wait_ge(e_add, 7 * c + m - 1)
                    w = CH[c % NC_][1]
                    pool.tensor_tensor(ssa[:, 0:w], ssa[:, 0:w], sqa[m % 2][:, 0:w], ALU.add).then_inc(e_add, 1)

            def add_h_squares(c, k):
                if k:
                    pool.wait_ge(n_sq, KD * c + k + 1)
                    if k > 1:
                        pool.wait_ge(n_add, 7 * c + k - 1)
                    w = CH[c][1]
                    pool.tensor_tensor(ssb[:, 0:w], ssb[:, 0:w], sqb[k % 2][:, 0:w], ALU.add).then_inc(n_add, 1)

            for st in range(NC_ + 1):
                if st:
                    c = st - 1
                    c0, w = CH[c]
                    pool.wait_ge(done, G_E + KD * st)
                    for r in range((w + P - 1) // P):
                        n = min(P, w - r * P)
                        src = I["x_prompt"][0, c0 + r * P:c0 + r * P + P, :] if c0 + r * P < SEQ \
                            else I["x_sample"].rearrange("b t n -> (b t) n")
                        pool.dma_start(xre[0:n, :, c0 + r * P:c0 + r * P + P] if n == P else
                                       xre_s[:, :, :], src.rearrange("p (k n) -> p k n", n=P)).then_inc(xr_in, 16)
                for m in range(KD):
                    if st < NC_:
                        add_product_squares(st, m)
                    if st and 1 <= m <= 4:
                        add_h_squares(st - 1, 2 * m - 2)
                        add_h_squares(st - 1, 2 * m - 1)
            for c in range(NC_):
                for m in range(KD):
                    add_product_squares(NC_ + c, m)
            pool.wait_ge(moved_out, 16 * 3)
            pool.wait_ge(rows_out, 16 * 4)
            pool.wait_ge(state_out, 16 * 2)

        @block.scalar
        def _(act):
            def split(n):
                act.wait_ge(raw_in[n % 2], RAW[n])
                if slot_free(n):
                    act.wait_ge(done, slot_free(n))
                act.activation(slot(n)[0], raw[:, n % 2, :], ACT.Copy).then_inc(w_hi, 1)

            def x_stats(r):
                n = P if r < NBLK else SROWS
                src = xrow[:, r, :] if r < NBLK else xrow_s[:, :]
                act.wait_ge(x_in[r], 16)
                if r:
                    act.wait_ge(x_sd, r)
                act.activation(xsq[0:n, :], src, ACT.Square, accum_out=ss[0:n, r:r + 1]).then_inc(x_ss, 1)
                act.wait_ge(x_ss, r + 1)
                act.activation(rs[0:n, r:r + 1], ss[0:n, r:r + 1], ACT.Sqrt, bias=eps[0:n], scale=1.0 / D).then_inc(x_sd, 1)

            def x_high(r):
                n = P if r < NBLK else SROWS
                act.wait_ge(x_t, r + 1)
                src = ps[:, 2 + 2 * (r % 2):4 + 2 * (r % 2), :].rearrange("p a (k n) -> p (a k) n", n=P)
                act.activation(xn[:, 0, :, r * P:r * P + n], src[:, :, 0:n], ACT.Copy).then_inc(x_hi, 1)

            def in_group(n, c):
                g = 3 * n + c
                c0, w = CH[c]
                b = vec[:, vcol(n):vcol(n) + 1]
                act.wait_ge(done, g + 1)
                src = ps[:, bank_of(g), 0:w]
                if n == U_V:
                    act.activation(vT[:, cs(c)], src, ACT.Identity, bias=b).then_inc(freed["A"], 1)
                elif n >= U_UP:
                    t = n - U_UP
                    np_ = min(w, SEQ - c0)
                    one = act.activation(upp[:, t, PSTATE + c0:PSTATE + c0 + np_], src[:, 0:np_], ACT.Identity, bias=b)
                    if w > np_:
                        one = act.activation(ups[:, t, :, PSTATE:],
                                             src[:, np_:w].rearrange("p (b s) -> p b s", s=T_DEC), ACT.Identity, bias=b)
                    one.then_inc(freed["A"], 1)
                else:
                    dst = kk[:, 0, cs(c)] if n == U_K else qo[:, 0, n - U_Q, cs(c)]
                    act.activation(dst, src, ACT.Identity, bias=b).then_inc(in_hi, 1)

            act.wait_ge(consts, 5)
            x_stats(0)
            for r in range(RT):
                if r + 1 < RT:
                    x_stats(r + 1)
                x_high(r)
                if r == 0:
                    split(U_K)
                if r == 1:
                    act.wait_ge(kc_t, 1)
                    act.activation(kxT[:, :, 0:WIN], ps[:, 6:8, :].rearrange("p a (b n) -> p (a b) n", n=P), ACT.Copy)\
                        .then_inc(kc_r, 1)
                    act.wait_ge(vec_r, 1)
                if r == 4:
                    in_group(U_K, 0)
                    split(U_V)
                if r == 7:
                    in_group(U_K, 1)
            in_group(U_K, 2)
            for n in range(U_V, U_UP):
                for c in range(NC_):
                    in_group(n, c)
                    if c == 0:
                        split(n + 1)
                    if n == U_Q and c == 0:
                        act.wait_ge(v_t, 1)
                        act.activation(vnew[:, :, :], ps[0:T_DEC, 6:8, :].rearrange("p a (b n) -> p (a b) n", n=P), ACT.Copy)\
                            .then_inc(vn_r, 1)
                        act.activation(kout[:, 0, :], ps[:, 4, 0:P], ACT.Copy).then_inc(ko_r, 1)
                        act.activation(kout[0:SROWS, 1, :], ps[0:SROWS, 4, P:2 * P], ACT.Copy).then_inc(ko_r, 1)
                    if n == U_Q + 1 and c == 0:
                        act.wait_ge(bias_p, 1)
                        act.activation(bias[:, :, :], ps[:, 4:8, :].rearrange("p a (b n) -> p (a b) n", n=2 * WIN), ACT.Copy)\
                            .then_inc(bias_r, 1)

            fill = 0
            for s in range(A_STEPS):
                u = s - 1
                if 0 <= u < A_UNITS:
                    act.wait_ge(pt_t, u + 1)
                    if u:
                        act.wait_ge(pv, u)
                    act.activation(pt[:, 0:4, :], ps[:, 4, :].rearrange("p (b n) -> p b n", n=P), ACT.Copy).then_inc(pt_a, 1)
                u = s
                if u < A_UNITS:
                    q, (k0, kw) = u % 2, keys(u)
                    act.wait_ge(stats, u + 1)
                    act.activation(stat[:, ES, u % 4, :], stat[:, DD, u % 4, :], ACT.Exp, scale=SCALE)
                    for i in range(4):
                        one = act.activation(pr[:, q, i, k0:k0 + kw], pr[:, q, i, k0:k0 + kw], ACT.Exp,
                                             bias=stat[:, NM, u % 4, i:i + 1], scale=SCALE,
                                             accum_out=stat[:, LL, u % 4, i:i + 1])
                    one.then_inc(expd, 1)
                if s >= 4 and s % 2 == 0:
                    b = (s - 4) // 2
                    act.wait_ge(o_t, b + 1)
                    if b < NBLK:
                        act.activation(qo[:, 0, :, b * P:(b + 1) * P], ps[:, 7, :].rearrange("p (i n) -> p i n", n=P),
                                       ACT.Copy).then_inc(o_hi, 1)
                    else:
                        for half in range(2):
                            dst, src = sample_out(0, half)
                            act.activation(dst, src, ACT.Copy).then_inc(o_hi, 1)
                if s in FILL:
                    n, c = U_UP + fill // NC_, fill % NC_
                    if fill == 0:
                        act.wait_ge(pads, 1)
                    in_group(n, c)
                    if c == 0:
                        split(n + 1)
                    fill += 1

            act.wait_ge(st_o, 1)
            act.activation(stout[0:PSTATE, 0, :], ps[0:PSTATE, 6, :], ACT.Copy).then_inc(st_or, 1)
            act.activation(stout[0:SROWS, 1, :], ps[0:SROWS, 7, :], ACT.Copy).then_inc(st_or, 1)
            act.wait_ge(rows_out, 16 * 4)
            for t in range(PT_):
                for c in range(NC_):
                    g = G_GRP + NC_ * t + c
                    act.wait_ge(done, g + 1)
                    act.activation(zz[:, 0, t, cs(c)], ps[:, bank_of(g), 0:CH[c][1]], ACT.Copy,
                                   scale=vec[:, V_PS + t:V_PS + t + 1]).then_inc(z_hi, 1)

            for j in range(KD):
                for x, dst in enumerate((sga, sgp)):
                    n = U_D + 3 * j + x
                    for c in range(NC_):
                        g = G_D + 12 * j + 3 * x + c
                        act.wait_ge(done, g + 1)
                        if j:
                            act.wait_ge(mixed, 3 * (j - 1) + c + 1)
                        act.activation(dst[:, cs(c)], ps[:, bank_of(g), 0:CH[c][1]], ACT.Sigmoid,
                                       bias=vec[:, 10 + KD * x + j:11 + KD * x + j]).then_inc(freed["A"], 1)
                        if c == 0:
                            split(n + 1)
                if j + 1 < KD:
                    act.wait_ge(done, G_D + 12 * j + 8)
                    split(U_D + 3 * j + 3)
            act.wait_ge(done, G_D + 12 * KD - 6)
            act.wait_ge(mixed, 3 * (KD - 1))
            for c in range(NC_):
                act.activation(xn[:, 0, 0:KD - 1, cs(c)], mix[:, 0:KD - 1, cs(c)], ACT.Copy).then_inc(m_hi, 1)
            for c in range(NC_):
                act.wait_ge(mixed, 3 * (KD - 1) + c + 1)
                act.activation(xn[:, 0, KD - 1, cs(c)], mix[:, KD - 1, cs(c)], ACT.Copy).then_inc(m_hi, 1)
            split(U_E)
            split(U_E + 1)

            def product_square(c, m, src):
                w = CH[c % NC_][1]
                if m == 0 and c:
                    act.wait_ge(n_sum, 2 * c - 1 if c <= NC_ else 2 * NC_ + c - NC_)
                if m >= 3:
                    act.wait_ge(e_add, 7 * c + m - 2)
                dst = ssa if m == 0 else sqa[m % 2]
                act.activation(dst[:, 0:w], src, ACT.Square).then_inc(e_sq, 1)

            def root(s, w):
                act.wait_ge(n_sum, s + 1)
                act.activation(rstd[:, 0:w], ps[:, 4, 0:w], ACT.Sqrt, bias=eps, scale=1.0 / D).then_inc(n_sd, 1)

            def norm_part(c, m):
                w = CH[c][1]
                if m == 0:
                    root(2 * c, w)
                elif m <= 4:
                    for k in (2 * m - 2, 2 * m - 1):
                        act.wait_ge(n_h, KD * c + k + 1)
                        if k == 0 and c == 0:
                            act.wait_ge(state_out, 16 * 2)
                        if k == 0 and c:
                            act.wait_ge(n2_lo, KD * c)
                        if k >= 3:
                            act.wait_ge(n_add, 7 * c + k - 2)
                        act.activation((ssb if k == 0 else sqb[k % 2])[:, 0:w], hh[:, k, cs(c)], ACT.Square).then_inc(n_sq, 1)
                elif m == 5:
                    root(2 * c + 1, w)
                else:
                    for k in range(4 * (m - 6), 4 * (m - 5)):
                        act.wait_ge(n2_t, KD * c + k + 1)
                        act.activation(xn[:, 0, k, cs(c)], sqb[k % 2][:, 0:w], ACT.Copy).then_inc(n2_hi, 1)

            def hidden(blk, j, c):
                g, e, w = g_up(blk, j, c), e_up(blk, j, c), CH[c][1]
                f = sqa[(NC_ * j + c if not isinstance(blk, int) else e) % 2][:, 0:w]
                act.wait_ge(done, g + 1)
                if isinstance(blk, int) and e < 2:
                    act.wait_ge(e_add, 7 * NC_)
                else:
                    act.wait_ge(f_lo, e - 1)
                act.activation(f, ps[:, bank_up(blk, j, c), 0:w], ACT.Relu).then_inc(freed["A"], 1)
                act.wait_ge(freed["A"], per_block(lambda b: FREED[g_up(b, j, c)][1], blk))
                act.activation(f, f, ACT.Square).then_inc(f_sq, 1)
                act.wait_ge(f_sq, e + 1)
                act.activation(ff[:, 0, j, cs(c)], f, ACT.Copy).then_inc(f_hi, 1)

            def split_mlp(blk, x):
                n = U_M + x
                act.wait_ge(raw_in[n % 2], per_block(lambda b: RAW[U_M + 8 * b + x], blk))
                act.wait_ge(done, per_block(lambda b: unit_end(U_M + 8 * b + x - 2), blk))
                act.activation(wr[:, n % 2, 0, :], raw[:, n % 2, :], ACT.Copy).then_inc(w_hi, 1)

            for st in range(NC_ + 1):
                for m in range(KD):
                    if st < NC_:
                        g = G_E + KD * st + m
                        act.wait_ge(done, g + 1)
                        product_square(st, m, ps[:, bank_of(g), 0:CH[st][1]])
                    else:
                        hidden(0, *STAGE3[m])
                    if st == 0 and m < 6:
                        split(U_E + 2 + m)
                    if st == 2 and 2 <= m < 2 + FB:
                        split(U_M + m - 2)
                    if st == 3 and m in (2, 3):
                        split(U_M + FB + m - 2)
                    if st:
                        norm_part(st - 1, m)
            for j in range(FB):
                hidden(0, j, 2)
            for x in (6, 7, 8):
                act.wait_ge(done, g_down(0, 2 * (x - 5), 0) + 1)
                split_mlp(0, x) if x < 8 else split_mlp(1, 0)

            def mlp_block(blk):
                for j, c in MAIN:
                    hidden(blk, j, c)
                    if c == 0:
                        split_mlp(blk, j + 1)
                for x in (5, 6, 7, 8):
                    act.wait_ge(done, per_block(lambda b: G_M + 36 * b + UP_G + 6 * (x - 5) + 1, blk))
                    split_mlp(blk, x) if x < 8 else split_mlp(blk + 1, 0)

            with act.Fori(1, LAST) as blk:
                mlp_block(blk)
            for j, c in MAIN:
                hidden(LAST, j, c)
                if c == 0:
                    split(U_M + 8 * LAST + j + 1)

            def y_part(c, m):
                if m == 0:
                    root(2 * NC_ + c, CH[c][1])
                elif m >= 5 and m - 5 < (CH[c][1] + P - 1) // P:
                    r = CH[c][0] // P + m - 5
                    n = min(P, ROWS - r * P)
                    act.wait_ge(y_p, r + 1)
                    act.activation(yrow[0:n, r, 0:D // 2], ps[0:n, 4 + 2 * (r % 2), :], ACT.Copy).then_inc(y_ra, 1)

            split(U_LASTD + 1)
            for st in range(NC_ + 1):
                for m in range(KD):
                    if st < NC_:
                        g = g_down(LAST, m, st)
                        act.wait_ge(freed["D"], FREED[g][1])
                        product_square(NC_ + st, m, acc[:, m, cs(st)])
                    if st == 0 and m in (0, 1):
                        split(U_LASTD + 2 + m)
                    if st:
                        y_part(st - 1, m)

        @block.vector
        def _(dve):
            def lo(n):
                dve.wait_ge(w_hi, n + 1)
                hi_, lo_ = slot(n)
                dve.tensor_tensor(lo_, raw[:, n % 2, :], hi_.bitcast(f32), ALU.subtract).then_inc(w_lo, 1)

            steps = [0]

            def chained(ins):
                steps[0] += 1
                ins.then_inc(dvs, 1)
                dve.wait_ge(dvs, steps[0])

            def x_scale(r):
                n = P if r < NBLK else SROWS
                x = xrow[:, r, :] if r < NBLK else xrow_s[:, :]
                dve.wait_ge(x_sd, r + 1)
                dve.reciprocal(rs[0:n, r:r + 1], rs[0:n, r:r + 1]).then_inc(x_rs, 1)
                dve.wait_ge(x_rs, r + 1)
                dve.scalar_tensor_tensor(out=x, in0=x, scalar=rs[0:n, r:r + 1], in1=gbc[0:n, :],
                                         op0=ALU.mult, op1=ALU.mult).then_inc(x_n, 1)

            def x_low(r):
                n = P if r < NBLK else SROWS
                dve.wait_ge(x_hi, r + 1)
                src = ps[:, 2 + 2 * (r % 2):4 + 2 * (r % 2), :].rearrange("p a (k n) -> p (a k) n", n=P)
                dve.tensor_tensor(xn[:, 1, :, r * P:r * P + n], src[:, :, 0:n],
                                  xn[:, 0, :, r * P:r * P + n].bitcast(f32), ALU.subtract).then_inc(x_lo, 1)

            his = [0]

            def in_group(n, c):
                g = 3 * n + c
                w = CH[c][1]
                b = vec[:, vcol(n):vcol(n) + 1]
                if n == U_V or n >= U_UP:
                    return
                his[0] += 1
                dve.wait_ge(in_hi, his[0])
                src = ps[:, bank_of(g), 0:w]
                dst = kk if n == U_K else qo[:, :, n - U_Q, :]
                if c == NC_ - 1:
                    new = src[:, w - SROWS:w]
                    if n == U_K:
                        dve.tensor_scalar(kf[:, :], src[:, w - SROWS - WIN:w], b, None, ALU.add).then_inc(kf_r, 1)
                        dve.wait_ge(kc_r, 1)
                        dve.tensor_scalar(kxT[:, :, WIN:], new.rearrange("p (b s) -> p b s", s=T_DEC), b, None, ALU.add)
                    else:
                        dve.tensor_scalar(qs[:, :, n - U_Q, :], new.rearrange("p (b s) -> p b s", s=T_DEC), b, None, ALU.add)
                dve.scalar_tensor_tensor(out=dst[:, 1, cs(c)], in0=src, scalar=b, in1=dst[:, 0, cs(c)].bitcast(f32),
                                         op0=ALU.add, op1=ALU.subtract).then_inc(freed["D"], 1)

            dve.wait_ge(vec_t, 1)
            dve.tensor_copy(vec[:, 0:62], ps[:, 6, 0:62]).then_inc(vec_r, 1)
            dve.wait_ge(consts, 5)
            dve.wait_ge(brow_p, 1)
            dve.tensor_scalar(brow[:, WIN:2 * WIN], ps[0:HEADS, 7, 0:P], 1.0 / SCALE, None, ALU.mult).then_inc(brow_r, 1)
            dve.wait_ge(gbc_in, 16)
            x_scale(0)
            for r in range(RT):
                if r + 1 < RT:
                    x_scale(r + 1)
                x_low(r)
                if r == 0:
                    lo(U_K)
                if r == 3:
                    dve.wait_ge(st_t, 1)
                    dve.tensor_copy(ups[:, :, :, 0:PSTATE],
                                    ps[:, 6, 0:PT_ * NB_DEC * PSTATE].rearrange("p (t b s) -> p t b s", t=PT_, b=NB_DEC))\
                        .then_inc(st_r, 1)
                if r == 4:
                    in_group(U_K, 0)
                    lo(U_V)
                if r == 7:
                    in_group(U_K, 1)
            in_group(U_K, 2)
            for n in range(U_V, U_UP):
                for c in range(NC_):
                    in_group(n, c)
                    if c == 0:
                        lo(n + 1)
                    if n == U_Q and c == 0:
                        dve.wait_ge(v_t, 1)
                        dve.tensor_copy(vr[:, :, :], ps[:, 2:4, :].rearrange("p a (b n) -> p (a b) n", n=P)).then_inc(v_r, 1)
                    if n == U_Q + 1 and c == 0:
                        dve.wait_ge(sb_p, 1)
                        chained(dve.tensor_copy(bias_s[:, :, :], ps[:, 3, 0:KVH * (KXW + 1)].rearrange("p (g n) -> p g n", g=KVH)))
                        dve.tensor_scalar(bias_s[:, :, KXW:], bias_s[:, :, KXW:], 1.0 / SCALE, None, ALU.mult)
                        chained(dve.tensor_scalar(sink[:, :], sink[:, :], 1.0 / SCALE, None, ALU.mult))

            fill = 0
            for s in range(A_STEPS):
                u = s
                if u < A_UNITS:
                    q, (k0, kw) = u % 2, keys(u)
                    if u == 0:
                        dve.wait_ge(bias_r, 1)
                    dve.wait_ge(qk, u + 1)
                    if u >= 2:
                        dve.wait_ge(pt_t, u - 1)
                    for i in range(4):
                        bi = bias_s[:, i // 2, 0:KXW] if u == A_UNITS - 1 else bias[:, GRP * (u % 2) + i, k0:k0 + kw]
                        one = dve.tensor_tensor_reduce(out=pr[:, q, i, k0:k0 + kw], in0=scores(i)[:, k0:k0 + kw], in1=bi,
                                                       scale=1.0, scalar=-3e38, op0=ALU.add, op1=ALU.max,
                                                       accum_out=stat[:, MX, u % 4, i:i + 1])
                    one.then_inc(s_free, 1)
                    dve.wait_ge(s_free, u + 1)
                    if u < A_UNITS - 1:
                        sk = sink[:, GRP * (u % 2):GRP * (u % 2) + GRP]
                        v4 = lambda x: stat[:, x, u % 4, :]
                    else:
                        sk = bias_s[:, :, KXW:].to_broadcast([P, KVH, 2])
                        v4 = lambda x: stat[:, x, u % 4, :].rearrange("p (g b) -> p g b", g=KVH)
                    chained(dve.tensor_tensor(v4(MM), v4(MX), sk, ALU.max))
                    chained(dve.tensor_tensor(v4(DD), sk, v4(MM), ALU.subtract))
                    dve.tensor_scalar(stat[:, NM, u % 4, :], stat[:, MM, u % 4, :], -SCALE, None, ALU.mult).then_inc(stats, 1)
                u = s - 1
                if 0 <= u < A_UNITS:
                    dve.wait_ge(pt_t, u + 1)
                    if u:
                        dve.wait_ge(pv, u)
                    dve.tensor_copy(pt[:, 4:8, :], ps[:, 5, :].rearrange("p (b n) -> p b n", n=P)).then_inc(pt_d, 1)
                u = s - 2
                if 0 <= u < A_UNITS:
                    q = u % 2
                    dve.wait_ge(expd, u + 1)
                    chained(dve.tensor_tensor(stat[:, RR, u % 4, :], stat[:, LL, u % 4, :], stat[:, ES, u % 4, :], ALU.add))
                    chained(dve.reciprocal(stat[:, RR, u % 4, :], stat[:, RR, u % 4, :]))
                    dve.wait_ge(pv, u + 1)
                    if u >= 2:
                        dve.wait_ge(o_t, u // 2)
                    if u < A_UNITS - 1:
                        dst, src = orow[:, :, u % 2, :], ps[:, 6, 0:4 * HD].rearrange("p (i d) -> p i d", d=HD)
                        rr = stat[:, RR, u % 4, :].unsqueeze(2).to_broadcast([P, 4, HD])
                    else:
                        dst = orow[:, 0:2, :, :].rearrange("p b g d -> p g b d")
                        src = ps[:, 6, 0:4 * HD].rearrange("p (g b d) -> p g b d", g=KVH, d=HD)
                        rr = stat[:, RR, u % 4, :].rearrange("p (g b) -> p g b", g=KVH).unsqueeze(3)\
                            .to_broadcast([P, KVH, 2, HD])
                    dve.tensor_tensor(dst, src, rr, ALU.mult).then_inc(o_norm, 1)
                if s >= 4 and s % 2 == 0:
                    b = (s - 4) // 2
                    if b < NBLK:
                        dve.wait_ge(o_hi, b + 1)
                        dve.tensor_tensor(qo[:, 1, :, b * P:(b + 1) * P], ps[:, 7, :].rearrange("p (i n) -> p i n", n=P),
                                          qo[:, 0, :, b * P:(b + 1) * P].bitcast(f32), ALU.subtract).then_inc(o_lo, 1)
                    else:
                        dve.wait_ge(o_hi, b + 2)
                        for half in range(2):
                            dst, src = sample_out(1, half)
                            hi_, _ = sample_out(0, half)
                            dve.tensor_tensor(dst, src, hi_.bitcast(f32), ALU.subtract).then_inc(o_lo, 1)
                if s in FILL:
                    n, c = U_UP + fill // NC_, fill % NC_
                    if c == 0:
                        lo(n + 1)
                    fill += 1

            for t in range(PT_):
                for c in range(NC_):
                    g = G_GRP + NC_ * t + c
                    dve.wait_ge(z_hi, NC_ * t + c + 1)
                    dve.scalar_tensor_tensor(out=zz[:, 1, t, cs(c)], in0=ps[:, bank_of(g), 0:CH[c][1]],
                                             scalar=vec[:, V_PS + t:V_PS + t + 1], in1=zz[:, 0, t, cs(c)].bitcast(f32),
                                             op0=ALU.mult, op1=ALU.subtract).then_inc(freed["D"], 1)

            def mix_group(j, c):
                w = CH[c][1]
                ga = G_D + 12 * j + 6 + 2 * c
                dve.wait_ge(done, ga + 2)
                dve.wait_ge(freed["A"], FREED[G_D + 12 * j + 3 + c][1])
                dve.tensor_tensor(sga[:, cs(c)], ps[:, bank_of(ga), 0:w], sga[:, cs(c)], ALU.mult).then_inc(freed["D"], 1)
                dve.tensor_tensor(sgp[:, cs(c)], ps[:, bank_of(ga + 1), 0:w], sgp[:, cs(c)], ALU.mult).then_inc(freed["D"], 1)
                dve.wait_ge(freed["D"], FREED[ga + 1][1])
                dve.tensor_tensor(mix[:, j, cs(c)], sga[:, cs(c)], sgp[:, cs(c)], ALU.add).then_inc(mixed, 1)

            def mix_low(c, k0, k1, count):
                dve.wait_ge(m_hi, count)
                dve.tensor_tensor(xn[:, 1, k0:k1, cs(c)], mix[:, k0:k1, cs(c)], xn[:, 0, k0:k1, cs(c)].bitcast(f32),
                                  ALU.subtract).then_inc(m_lo, 1)

            for j in range(KD):
                n = U_D + 3 * j
                lo(n + 1)
                lo(n + 2)
                for c in range(NC_):
                    if j == KD - 1 and c:
                        mix_low(c - 1, 0, KD - 1, c)
                    mix_group(j, c)
                    if c == 0 and j + 1 < KD:
                        lo(n + 3)
            mix_low(0, KD - 1, KD, NC_ + 1)
            mix_low(2, 0, KD - 1, NC_)
            mix_low(1, KD - 1, KD, NC_ + 2)
            mix_low(2, KD - 1, KD, NC_ + 3)
            lo(U_E)
            lo(U_E + 1)

            def invert(s, w):
                dve.wait_ge(n_sd, s + 1)
                dve.reciprocal(rstd[:, 0:w], rstd[:, 0:w]).then_inc(n_rs, 1)
                dve.wait_ge(n_rs, s + 1)

            def norm_part(c, m):
                w = CH[c][1]
                if m == 0:
                    invert(2 * c, w)
                elif m <= 4:
                    for k in (2 * m - 2, 2 * m - 1):
                        h = hh[:, k, cs(c)]
                        dve.scalar_tensor_tensor(out=h, in0=h, scalar=vec[:, V_G1 + k:V_G1 + k + 1], in1=rstd[:, 0:w],
                                                 op0=ALU.mult, op1=ALU.mult).then_inc(n_t, 1)
                    for k in (2 * m - 2, 2 * m - 1):
                        h = hh[:, k, cs(c)]
                        dve.wait_ge(n_t, KD * c + k + 1)
                        dve.wait_ge(xr_t, KD * c + k + 1)
                        dve.tensor_tensor(h, h, ps[:, 5 + k % 2, 0:w], ALU.add).then_inc(n_h, 1)
                elif m == 5:
                    invert(2 * c + 1, w)
                else:
                    for k0 in (4 * (m - 6), 4 * (m - 6) + 2):
                        for k in (k0, k0 + 1):
                            if k >= 2:
                                dve.wait_ge(n2_lo, KD * c + k - 1)
                            dve.scalar_tensor_tensor(out=sqb[k % 2][:, 0:w], in0=hh[:, k, cs(c)],
                                                     scalar=vec[:, V_G2 + k:V_G2 + k + 1], in1=rstd[:, 0:w],
                                                     op0=ALU.mult, op1=ALU.mult).then_inc(n2_t, 1)
                        for k in (k0, k0 + 1):
                            dve.wait_ge(n2_hi, KD * c + k + 1)
                            dve.tensor_tensor(xn[:, 1, k, cs(c)], sqb[k % 2][:, 0:w], xn[:, 0, k, cs(c)].bitcast(f32),
                                              ALU.subtract).then_inc(n2_lo, 1)

            def hidden_low(blk, j, c):
                e, w = e_up(blk, j, c), CH[c][1]
                f = sqa[(NC_ * j + c if not isinstance(blk, int) else e) % 2][:, 0:w]
                dve.wait_ge(f_hi, e + 1)
                dve.tensor_tensor(ff[:, 1, j, cs(c)], f, ff[:, 0, j, cs(c)].bitcast(f32), ALU.subtract).then_inc(f_lo, 1)

            def lo_mlp(blk, x):
                n = U_M + x
                dve.wait_ge(w_hi, blk * 8 + (n + 1))
                dve.tensor_tensor(wr[:, n % 2, 1, :], raw[:, n % 2, :], wr[:, n % 2, 0, :].bitcast(f32), ALU.subtract)\
                    .then_inc(w_lo, 1)

            def gather(blk, m, c):
                g, w = g_down(blk, m, c), CH[c][1]
                dve.wait_ge(done, g + 1)
                src = ps[:, bank_down(blk, m, c), 0:w]
                a = acc[:, m, cs(c)]
                if is_block(blk, 0):
                    dve.tensor_copy(a, src).then_inc(freed["D"], 1)
                else:
                    dve.tensor_tensor(a, a, src, ALU.add).then_inc(freed["D"], 1)

            for st in range(NC_ + 1):
                for m in range(KD):
                    if st < NC_:
                        g = G_E + KD * st + m
                        dve.wait_ge(e_sq, KD * st + m + 1)
                        dve.tensor_copy(hh[:, m, cs(st)], ps[:, bank_of(g), 0:CH[st][1]]).then_inc(freed["D"], 1)
                    else:
                        hidden_low(0, *STAGE3[m])
                    if st == 0 and m < 6:
                        lo(U_E + 2 + m)
                    if st == 2 and 2 <= m < 2 + FB:
                        lo(U_M + m - 2)
                    if st == 3 and m in (2, 3):
                        lo(U_M + FB + m - 2)
                    if st:
                        if m == 0:
                            dve.wait_ge(freed["D"], FREED[G_E + KD * st - 1][1])
                        norm_part(st - 1, m)
            for j in range(FB):
                hidden_low(0, j, 2)
            for m, c in DOWN:
                gather(0, m, c)
                if m % 2 == 0 and m and c == 0:
                    x = FB + m // 2 + 1
                    lo_mlp(0, x) if x < 8 else lo_mlp(1, 0)

            def mlp_block(blk):
                for j, c in MAIN:
                    hidden_low(blk, j, c)
                    if c == 0:
                        lo_mlp(blk, j + 1)
                for m, c in DOWN:
                    gather(blk, m, c)
                    if m % 2 == 0 and c == 0:
                        x = FB + m // 2 + 1
                        lo_mlp(blk, x) if x < 8 else lo_mlp(blk + 1, 0)

            with dve.Fori(1, LAST) as blk:
                mlp_block(blk)
            for j, c in MAIN:
                hidden_low(LAST, j, c)
                if c == 0:
                    lo(U_M + 8 * LAST + j + 1)
            lo(U_LASTD + 1)

            def y_part(c, m):
                w = CH[c][1]
                if m == 0:
                    invert(2 * NC_ + c, w)
                elif m <= 4:
                    for k in (2 * m - 2, 2 * m - 1):
                        a = acc[:, k, cs(c)]
                        dve.scalar_tensor_tensor(out=a, in0=a, scalar=vec[:, V_G3 + k:V_G3 + k + 1], in1=rstd[:, 0:w],
                                                 op0=ALU.mult, op1=ALU.mult).then_inc(y_t, 1)
                    for k in (2 * m - 2, 2 * m - 1):
                        dve.wait_ge(y_t, KD * c + k + 1)
                        h = hh[:, k, cs(c)]
                        dve.tensor_tensor(h, h, acc[:, k, cs(c)], ALU.add).then_inc(y_h, 1)
                elif m - 5 < (w + P - 1) // P:
                    r = CH[c][0] // P + m - 5
                    n = min(P, ROWS - r * P)
                    dve.wait_ge(y_p, r + 1)
                    dve.tensor_copy(yrow[0:n, r, D // 2:D], ps[0:n, 5 + 2 * (r % 2), :]).then_inc(y_rd, 1)

            for st in range(NC_ + 1):
                for m in range(KD):
                    if st < NC_:
                        gather(LAST, m, st)
                    if st == 0 and m in (0, 1):
                        lo(U_LASTD + 2 + m)
                    if st:
                        y_part(st - 1, m)

        @block.tensor
        def _(pe):
            def need(n):
                pe.wait_ge(w_lo, n + 1)

            def bank_free(g):
                q = before_in_bank(g)
                if q >= 0:
                    pe.wait_ge(freed[FREED[q][0]], FREED[q][1])

            def products(out, terms, inc):
                last = len(terms) - 1
                for i, ((wh, wl), (rh, rl)) in enumerate(terms):
                    pe.matmul(out, wh, rh, start=(i == 0), stop=False)
                    pe.matmul(out, wh, rl, start=False, stop=False)
                    mm = pe.matmul(out, wl, rh, start=False, stop=(i == last))
                if inc:
                    mm.then_inc(done, 1)

            def wtile(n, k, sl=slot):
                h, l = sl(n)
                return h[:, k * P:(k + 1) * P], l[:, k * P:(k + 1) * P]

            def rows(t, k, c):
                return t[:, 0, k, cs(c)], t[:, 1, k, cs(c)]

            def full_group(g, n, c):
                bank_free(g)
                products(ps[:, bank_of(g), 0:CH[c][1]], [(wtile(n, k), rows(xn, k, c)) for k in range(KD)], True)

            def turn(out, src, n=P):
                return pe.transpose(out, src, ident[0:n, 0:n])

            def x_turn(r):
                n = P if r < NBLK else SROWS
                pe.wait_ge(x_n, r + 1)
                if r >= 2:
                    pe.wait_ge(x_lo, r - 1)
                for k in range(KD):
                    src = xrow[:, r, k * P:(k + 1) * P] if r < NBLK else xrow_s[:, k * P:(k + 1) * P]
                    mm = turn(ps[:, 2 + 2 * (r % 2) + k // 4, (k % 4) * P:(k % 4) * P + n], src, n)
                mm.then_inc(x_t, 1)

            pe.wait_ge(consts, 5)
            pe.wait_ge(tab_in, 32)
            pe.matmul(ps[0:HEADS, 7, 0:P], table[:, :], onehot[:, :], start=True, stop=True).then_inc(brow_p, 1)
            pe.wait_ge(vec_in, 16 * 8)
            turn(ps[:, 6, 0:62], vecrow[:, :], 62).then_inc(vec_t, 1)
            x_turn(0)
            x_turn(1)
            pe.wait_ge(vec_r, 1)
            pe.wait_ge(brow_r, 1)
            pe.wait_ge(kc_in, 16)
            for b in range(NB_DEC):
                mm = turn(ps[:, 6 + b // 4, (b % 4) * P:(b % 4 + 1) * P], kcache[:, b, :])
            mm.then_inc(kc_t, 1)
            x_turn(2)
            x_turn(3)
            pe.wait_ge(kc_r, 1)
            pe.wait_ge(st_in, 16)
            for t in range(PT_):
                ns = NB_DEC * PSTATE
                mm = turn(ps[:, 6, t * ns:(t + 1) * ns], state_in[:, t * P:(t + 1) * P], ns)
            mm.then_inc(st_t, 1)
            for c in range(NC_):
                need(U_K)
                pe.wait_ge(x_lo, min(3 * c + 3, RT))
                full_group(3 * U_K + c, U_K, c)
                for r in range(4 + 3 * c, min(7 + 3 * c, RT)):
                    x_turn(r)
            need(U_V)
            for c in range(NC_):
                full_group(3 * U_V + c, U_V, c)
            for n in range(U_Q, U_UP):
                need(n)
                for c in range(NC_):
                    full_group(3 * n + c, n, c)
                    if n == U_Q and c == 0:
                        pe.wait_ge(freed["A"], FREED[3 * U_V + 2][1])
                        pe.wait_ge(st_r, 1)
                        pe.wait_ge(x_lo, RT)
                        pe.wait_ge(kf_r, 1)
                        for b in range(NBLK):
                            turn(ps[:, 2 + b // 4, (b % 4) * P:(b % 4 + 1) * P], vT[:, b * P:(b + 1) * P])
                        for b in range(NB_DEC):
                            turn(ps[0:T_DEC, 6 + b // 4, (b % 4) * P:(b % 4 + 1) * P],
                                 vT[:, SEQ + b * T_DEC:SEQ + (b + 1) * T_DEC])
                        turn(ps[:, 4, 0:P], kf[:, 0:WIN])
                        turn(ps[0:SROWS, 4, P:2 * P], kf[:, WIN:]).then_inc(v_t, 1)
                    if n == U_Q + 1 and c == 0:
                        pe.wait_ge(v_r, 1)
                        pe.wait_ge(vn_r, 1)
                        pe.wait_ge(ko_r, 2)
                        pe.wait_ge(rev_in, 16)
                        for i in range(4):
                            mm = pe.matmul(ps[:, 4 + i, :], anti[:, :], bias_rev[:, 2 * i:2 * i + 2, :], start=True, stop=True)
                        mm.then_inc(bias_p, 1)
                        pe.wait_ge(src_in, 16 * 10)
                        pe.matmul(ps[:, 3, 0:KVH * (KXW + 1)], perm_s[:, :], src_s[:, :, :], start=True, stop=True)\
                            .then_inc(sb_p, 1)

            def score_products(u):
                if u == 0:
                    pe.wait_ge(freed["D"], FREED[3 * U_UP - 1][1])
                    pe.wait_ge(dvs, 2)
                if u:
                    pe.wait_ge(s_free, u)
                if u < A_UNITS - 1:
                    b, g = divmod(u, 2)
                    lane, (k0, kw) = slice(g * HD, (g + 1) * HD), keys(u)
                    kc = slice((b - 1) * P + k0, (b - 1) * P + k0 + kw)
                    for i in range(GRP):
                        q_ = [qo[lane, x, i, b * P:(b + 1) * P] for x in range(2)]
                        k_ = [kk[lane, x, kc] for x in range(2)]
                        out = scores(i)[:, k0:k0 + kw]
                        pe.matmul(out, q_[0], k_[0], start=True, stop=False)
                        pe.matmul(out, q_[0], k_[1], start=False, stop=False)
                        mm = pe.matmul(out, q_[1], k_[0], start=False, stop=True)
                else:
                    for b in range(NB_DEC):
                        for g in range(KVH):
                            lane, part = slice(g * HD, (g + 1) * HD), slice(32 * (b % 4), 32 * (b % 4) + 32)
                            mm = pe.matmul(scores(2 * g + b // 4)[part, 0:KXW], qs[lane, b, :, :].rearrange("p i t -> p (i t)"),
                                           kxT[lane, b, :], start=True, stop=True)
                mm.then_inc(qk, 1)

            def turn_probs(u):
                pe.wait_ge(expd, u + 1)
                if u:
                    pe.wait_ge(pt_a, u)
                    pe.wait_ge(pt_d, u)
                else:
                    pe.wait_ge(bias_r, 1)
                k0, kw = keys(u)
                for i in range(4):
                    for h in range(2):
                        a, n = h * WIN, min(WIN, k0 + kw - h * WIN)
                        if a < k0:
                            a = WIN
                        mm = turn(ps[0:n, 4 + i // 2, ((2 * i + h) % 4) * P:((2 * i + h) % 4 + 1) * P], pr[:, u % 2, i, a:a + n])
                mm.then_inc(pt_t, 1)

            def weigh_values(u):
                pe.wait_ge(pt_a, u + 1)
                pe.wait_ge(pt_d, u + 1)
                if u:
                    pe.wait_ge(o_norm, u)
                if u < A_UNITS - 1:
                    b, g = divmod(u, 2)
                    for i in range(GRP):
                        for h in range(2):
                            if b + h:
                                mm = pe.matmul(ps[:, 6, i * HD:(i + 1) * HD], pt[:, 2 * i + h, :],
                                               vr[:, b - 1 + h, g * HD:(g + 1) * HD],
                                               start=(h == 0 or b == 0), stop=(h == 1))
                else:
                    pe.wait_ge(late_in, 16 * 3)
                    for b in range(NB_DEC):
                        for g in range(KVH):
                            x, part = 2 * g + b // 4, slice(32 * (b % 4), 32 * (b % 4) + 32)
                            out = ps[part, 6, x * HD:(x + 1) * HD]
                            pe.matmul(out, pt[:, 2 * x, part], vcache[:, b, g * HD:(g + 1) * HD], start=True, stop=False)
                            mm = pe.matmul(out, pt[0:T_DEC, 2 * x + 1, part], vnew[:, b, g * HD:(g + 1) * HD],
                                           start=False, stop=True)
                mm.then_inc(pv, 1)

            def turn_outputs(b):
                pe.wait_ge(o_norm, min(2 * b + 2, A_UNITS))
                if b:
                    pe.wait_ge(o_lo, b)
                for i in range(GRP if b < NBLK else 2):
                    mm = turn(ps[:, 7, i * P:(i + 1) * P], orow[:, i, :, :].rearrange("p g d -> p (g d)"))
                mm.then_inc(o_t, 1)

            fill = 0
            for s in range(A_STEPS):
                if s < A_UNITS:
                    score_products(s)
                if 0 <= s - 1 < A_UNITS:
                    turn_probs(s - 1)
                if s >= 4 and s % 2 == 0:
                    turn_outputs((s - 4) // 2)
                if 0 <= s - 2 < A_UNITS:
                    weigh_values(s - 2)
                if s in FILL:
                    n, c = U_UP + fill // NC_, fill % NC_
                    need(n)
                    full_group(3 * n + c, n, c)
                    fill += 1

            pe.wait_ge(pooled, PT_)
            pe.wait_ge(o_lo, NBLK + 2)
            for t in range(PT_):
                turn(ps[0:PSTATE, 6, t * P:(t + 1) * P], tails[:, t, 0:PSTATE])
            for t in range(PT_):
                mm = turn(ps[0:SROWS, 7, t * P:(t + 1) * P], tails[:, t, PSTATE:])
            mm.then_inc(st_o, 1)
            for t in range(PT_):
                for c in range(NC_):
                    g = G_GRP + NC_ * t + c
                    bank_free(g)
                    c0, w = CH[c]
                    np_ = min(w, SEQ - c0)
                    mm = pe.matmul(ps[:, bank_of(g), 0:np_], wgrp[:, t, :], upp[:, t, PSTATE + c0:PSTATE + c0 + np_],
                                   start=True, stop=True)
                    if w > np_:
                        mm = pe.matmul(ps[:, bank_of(g), np_:w], wgrp[:, t, :], ups[:, t, :, PSTATE:], start=True, stop=True)
                    mm.then_inc(done, 1)

            for j in range(KD):
                n, g = U_D + 3 * j, G_D + 12 * j
                for x in range(2):
                    need(n + x)
                    for c in range(NC_):
                        full_group(g + 3 * x + c, n + x, c)
                need(n + 2)
                if j == 0:
                    pe.wait_ge(freed["D"], FREED[G_D - 1][1])
                for c in range(NC_):
                    for x, t in enumerate((qo, zz)):
                        gg = g + 6 + 2 * c + x
                        bank_free(gg)
                        products(ps[:, bank_of(gg), 0:CH[c][1]],
                                 [(wtile(n + 2, 4 * x + k), rows(t, k, c)) for k in range(4)], True)

            def feature_sum(s, src, w):
                if s:
                    pe.wait_ge(n_sd, s)
                pe.matmul(ps[:, 4, 0:w], ones[:, :], src[:, 0:w], start=True, stop=True).then_inc(n_sum, 1)

            def norm_part(c, m):
                c0, w = CH[c]
                if m == 0:
                    pe.wait_ge(e_add, 7 * (c + 1))
                    feature_sum(2 * c, ssa, w)
                elif m <= 4:
                    for k in (2 * m - 2, 2 * m - 1):
                        if k == 0:
                            pe.wait_ge(xr_in, 16 * min(3 * c + 3, RT))
                        if KD * c + k >= 2:
                            pe.wait_ge(n_h, KD * c + k - 1)
                        for r in range((w + P - 1) // P):
                            n = min(P, w - r * P)
                            src = xre[:, k, c0 + r * P:c0 + r * P + P] if n == P else xre_s[:, k, :]
                            mm = turn(ps[:, 5 + k % 2, r * P:r * P + n], src, n)
                        mm.then_inc(xr_t, 1)
                elif m == 5:
                    pe.wait_ge(n_add, 7 * (c + 1))
                    feature_sum(2 * c + 1, ssb, w)

            def up_group(blk, j, c, n):
                g = g_up(blk, j, c)
                if isinstance(blk, int):
                    bank_free(g)
                    h, l = slot(n)
                else:
                    q1 = before_in_bank(g_up(1, j, c))
                    assert FREED[q1][0] == FREED[before_in_bank(g_up(2, j, c))][0]
                    pe.wait_ge(freed[FREED[q1][0]], per_block(lambda b: FREED[before_in_bank(g_up(b, j, c))][1], blk))
                    h, l = wr[:, n % 2, 0, :], wr[:, n % 2, 1, :]
                products(ps[:, bank_up(blk, j, c), 0:CH[c][1]],
                         [((h[:, k * P:(k + 1) * P], l[:, k * P:(k + 1) * P]), rows(xn, k, c)) for k in range(KD)], True)

            def down_group(blk, m, c, n):
                g = g_down(blk, m, c)
                if isinstance(blk, int):
                    bank_free(g)
                    h, l = slot(n)
                else:
                    q1 = before_in_bank(g_down(1, m, c))
                    pe.wait_ge(freed[FREED[q1][0]], per_block(lambda b: FREED[before_in_bank(g_down(b, m, c))][1], blk))
                    h, l = wr[:, n % 2, 0, :], wr[:, n % 2, 1, :]
                a = [slice(k * 2 * P + (m % 2) * P, k * 2 * P + (m % 2) * P + P) for k in range(FB)]
                products(ps[:, bank_down(blk, m, c), 0:CH[c][1]], [((h[:, a[k]], l[:, a[k]]), rows(ff, k, c)) for k in range(FB)], True)

            for st in range(NC_ + 1):
                for m in range(KD):
                    if st < NC_:
                        if m == 0:
                            pe.wait_ge(m_lo, (3, 5, 6)[st])
                        if st == 0:
                            need(U_E + m)
                        full_group(G_E + KD * st + m, U_E + m, st)
                    else:
                        j, c = STAGE3[m]
                        if c == 0:
                            need(U_M + j)
                        if j == 0:
                            pe.wait_ge(n2_lo, KD * (c + 1))
                        up_group(0, j, c, U_M + j)
                    if st:
                        norm_part(st - 1, m)
            pe.wait_ge(n2_lo, KD * NC_)
            for j in range(FB):
                up_group(0, j, 2, U_M + j)
            for m, c in DOWN:
                if m % 2 == 0 and c == 0:
                    need(U_M + FB + m // 2)
                if m == 0:
                    pe.wait_ge(f_lo, e_up(0, FB - 1, c) + 1)
                down_group(0, m, c, U_M + FB + m // 2)

            def mlp_block(blk):
                for j, c in MAIN:
                    if c == 0:
                        pe.wait_ge(w_lo, blk * 8 + (U_M + j + 1))
                    up_group(blk, j, c, U_M + j)
                for m, c in DOWN:
                    if m % 2 == 0 and c == 0:
                        pe.wait_ge(w_lo, blk * 8 + (U_M + FB + m // 2 + 1))
                    if m == 0:
                        pe.wait_ge(f_lo, e_up(blk, FB - 1, c) + 1)
                    down_group(blk, m, c, U_M + FB + m // 2)

            with pe.Fori(1, LAST) as blk:
                mlp_block(blk)
            for j, c in MAIN:
                n = U_M + 8 * LAST + j
                if c == 0:
                    need(n)
                up_group(LAST, j, c, n)

            def y_part(c, m):
                c0, w = CH[c]
                if m == 0:
                    pe.wait_ge(e_add, 7 * (NC_ + c + 1))
                    if c:
                        pe.wait_ge(y_ra, c0 // P)
                    feature_sum(2 * NC_ + c, ssa, w)
                elif m >= 5 and m - 5 < (w + P - 1) // P:
                    r = c0 // P + m - 5
                    n = min(P, ROWS - r * P)
                    pe.wait_ge(y_h, KD * (c + 1))
                    pe.wait_ge(n_sd, 2 * NC_ + c + 1)
                    if r >= 2:
                        pe.wait_ge(y_ra, r - 1)
                        pe.wait_ge(y_rd, r - 1)
                    for k in range(KD):
                        mm = turn(ps[0:n, 4 + 2 * (r % 2) + k // 4, (k % 4) * P:(k % 4 + 1) * P],
                                  hh[:, k, r * P:r * P + n])
                    mm.then_inc(y_p, 1)

            for st in range(NC_ + 1):
                for m in range(KD):
                    if st < NC_:
                        n = U_LASTD + m // 2
                        if st == 0 and m % 2 == 0:
                            need(n)
                        if m == 0:
                            pe.wait_ge(f_lo, e_up(LAST, FB - 1, st) + 1)
                        down_group(LAST, m, st, n)
                    if st:
                        y_part(st - 1, m)


def bucket_onehot():
    half = BUCKETS // 2
    out = np.zeros((BUCKETS, WIN), np.float32)
    for n in range(WIN):
        d = WIN - 1 - n
        b = d if d < half else min(BUCKETS - 1, half + int(math.log(d / half) / math.log(MAXD / half) * (BUCKETS - half)))
        out[b, n] = 1.0
    return out


def query_perm():
    out = np.zeros((32, P), np.float32)
    for p in range(P):
        i, t = (p // T_DEC) % GRP, p % T_DEC
        out[i * T_DEC + T_DEC - 1 - t, p] = 1.0
    return out


def inv_count():
    return np.array([[1.0 / min(n + 1, 2 ** (t + 1)) for t in range(PT_) for n in range(16)]], np.float32)


_INS = ["x_prompt", "x_sample", "cache_k_win", "cache_v_win", "state_pool", "norm_pre_mix", "norm_post_mix",
        "norm_pre_mlp", "norm_post_mlp", "w_in", "b_in", "attn_sinks", "rel_bias_table", "w_attn_up", "w_pool_grp",
        "pool_scale", "w_pool_up", "w_out", "w_mlp_up", "w_mlp_down"]
_OUTS = [("y_prompt", (1, SEQ, D)), ("y_sample", (NB_DEC, T_DEC, D)),
         ("k_win_prompt", (1, 1, WIN, KVH, HD)), ("v_win_prompt", (1, 1, WIN, KVH, HD)),
         ("pool_state_prompt", (1, 1, PSTATE, PW)),
         ("k_win_sample", (1, NB_DEC, WIN, KVH, HD)), ("v_win_sample", (1, NB_DEC, WIN, KVH, HD)),
         ("pool_state_sample", (1, NB_DEC, PSTATE, PW))]


def kernel(**inputs):
    import numpy as _np
    import concourse.bacc as _bacc
    from concourse import mybir as _mybir
    from concourse.bass_utils import run_bass_kernel_spmd as _run

    nc = _bacc.Bacc("TRN2", target_bir_lowering=False, num_devices=1)
    arrays, ins, outs = {}, {}, {}
    given = {name: _np.ascontiguousarray(inputs[name]) for name in _INS}
    given.update(bucket_onehot=bucket_onehot(), query_perm=query_perm(), inv_count=inv_count())
    for name, a in given.items():
        arrays[f"in_{name}"] = a
        ins[name] = nc.dram_tensor(f"in_{name}", a.shape, _mybir.dt.from_np(a.dtype), kind="ExternalInput").ap()
    for name, shape in _OUTS:
        outs[name] = nc.dram_tensor(f"out_{name}", shape, _mybir.dt.float32, kind="ExternalOutput").ap()
    build(nc, ins, outs)
    r = _run(nc, [arrays], core_ids=[0])
    return tuple(r.results[0][f"out_{name}"] for name, _ in _OUTS)
```

```python
import math
from contextlib import ExitStack

import numpy as np
import concourse.bass as bass
from concourse import mybir

D = 1024
SEQ = 1024
NB_DEC, T_DEC = 8, 8
SROWS = NB_DEC * T_DEC
ROWS = SEQ + SROWS
P = 128
KD = D // P
HEADS, HD, KVH = 8, 64, 2
GRP = HEADS // KVH
KVW = KVH * HD
AW = HEADS * HD
WIN = 128
PW = D // 2
PT_ = PW // P
PSTATE = 15
DFF = 4 * D
BUCKETS, MAXD = 32, 128
EPS = 1e-6
NEG = -1e30
COL_K, COL_V, COL_UP = AW, AW + KVW, AW + 2 * KVW
COL_GA, COL_GP = COL_UP + PW, COL_UP + PW + D
CH = [(0, 384), (384, 384), (768, ROWS - 768)]
NC_ = len(CH)
NBLK = SEQ // P
RT = NBLK + 1
KXW = WIN + T_DEC
FB = 4
NFB = DFF // (FB * P)
FY = 3 * P
SCALE = HD ** -0.5

U_K, U_V, U_Q, U_UP = 0, 1, 2, 6
U_D = 10
U_E = U_D + 3 * KD
U_M = U_E + KD
N_UNITS = U_M + 8 * NFB

G_GATE0 = 3 * U_D
G_GRP = G_GATE0 + 6
G_D = G_GATE0 + 3 * PT_
G_E = G_D + 12 * KD
G_M = G_E + 3 * KD
UP_G, DOWN_G = 3 * FB, 3 * KD
N_GROUPS = G_M + (UP_G + DOWN_G) * NFB
LAST = NFB - 1
BLOCK0 = [("up", j, c) for c in range(2) for j in range(FB)] + [("down", 0, 0), ("down", 1, 0), ("down", 0, 1)] \
    + [("up", j, 2) for j in range(FB)] + [("down", 1, 1), ("down", 0, 2), ("down", 1, 2)] \
    + [("down", m, c) for m in range(2, KD) for c in range(3)]


def g_in(n, c):
    return 2 * c + n if n < U_Q else 3 * n + c


def g_gate(j, x, c):
    return (G_GATE0 if j == 0 else G_D + 12 * j) + 3 * x + c


def mix_order(j):
    return [(0, 0), (1, 0), (0, 1), (2, 0), (1, 1), (2, 1)] if j == 0 else [(c, x) for c in range(NC_) for x in range(2)]


def g_mix(j, c, x):
    return G_D + 12 * j + 6 + mix_order(j).index((c, x))


def group_reader(g):
    if g < 3 * U_Q:
        return "DA"[g % 2]
    if g < G_GATE0:
        return "A" if g >= 3 * U_UP else "D"
    if g < G_GRP:
        return "A"
    if g < G_D + 12:
        return "D"
    if g < G_E:
        return "A" if (g - G_D) % 12 < 6 else "D"
    if g < G_M:
        return "A"
    if g < G_M + UP_G + DOWN_G:
        return "A" if BLOCK0[g - G_M][0] == "up" else "D"
    return "A" if (g - G_M) % (UP_G + DOWN_G) < UP_G else "D"


FREED = []
_n = {"A": 0, "D": 0}
for _g in range(N_GROUPS):
    _e = group_reader(_g)
    _n[_e] += 1
    FREED.append((_e, _n[_e]))


def unit_end(n):
    if n < U_D:
        return g_in(n, 2) + 1
    if n < U_E:
        j, x = divmod(n - U_D, 3)
        return g_gate(j, x, 2) + 1 if x < 2 else g_mix(j, 2, 1) + 1
    if n < U_M:
        return G_E + 2 * KD + (n - U_E) + 1
    blk, x = divmod(n - U_M, 8)
    base = G_M + (UP_G + DOWN_G) * blk
    if x < FB:
        return base + (BLOCK0.index(("up", x, 2)) + 1 if blk == 0 else 3 * x + 3)
    v = x - FB
    return base + UP_G + (2 * KD + 2 * v + 2 if blk == LAST else 6 * v + 6)


def per_block(value_of, blk):
    if isinstance(blk, int):
        return value_of(blk)
    v1, v2 = value_of(1), value_of(2)
    return blk * (v2 - v1) + (2 * v1 - v2)


YCH = [(0, 512), (512, 384), (896, ROWS - 896)]

A_UNITS = 4 * GRP + 1
A_STEPS = A_UNITS + 3
FILL = NC_ * (U_D - U_Q - 1)
assert FILL == A_STEPS + 1


def filler(i):
    return U_Q + 1 + i // NC_, i % NC_


def build(nc, I, O):
    f32, f32r = mybir.dt.float32, mybir.dt.float32r
    ALU, ACT = mybir.AluOpType, mybir.ActivationFunctionType
    ctx = ExitStack()
    with ctx:
        T = ROWS * 4

        def at(name, shape, off, dt=f32):
            return nc.alloc_sbuf_tensor_at(name, shape, dt, offset=16512 + off)

        XN, R16, R24, R32 = 0, 16 * T, 24 * T, 32 * T
        A1 = R16 + 19584
        A2 = R32 + 18432
        A3 = 40 * T
        CON = A3 + 8704
        RING = CON + 5472

        xn = at("xn", [P, 2, KD, ROWS], XN, f32r)
        xrow = at("xrow", [P, NBLK, D], R24)
        xrow_s = at("xrow_s", [SROWS, D], A2 + 5120)
        gbc = at("gbc", [P, D], A2 + 9216)
        xsq = at("xsq", [P, D], A2)
        anti = at("anti", [P, P], A2 + 4096)
        rs = at("rs", [P, RT], A2 + 4608)
        ss = at("ss", [P, RT], RING - 64)
        bias_rev = at("bias_rev", [P, HEADS, 2 * WIN], R16)
        kcache = at("kcache", [P, NB_DEC, KVW], R16 + 8192)
        state_in = at("state_in", [NB_DEC * PSTATE, PW], R16 + 12288)
        brow = at("brow", [HEADS, FY], R16 + 14336)
        onehot = at("onehot", [BUCKETS, P], R16 + 15872)
        table = at("table", [BUCKETS, HEADS], R16 + 16384)
        upp = at("upp", [P, PT_, PSTATE + SEQ], R16)
        ups = at("ups", [P, PT_, NB_DEC, PSTATE + T_DEC], R16 + 16640)
        bias = at("bias", [P, HEADS, 2 * WIN], A1)
        orow = at("orow", [P, 2, KVH, HD], A1 + 8192)
        wgrp = at("wgrp", [P, PT_, P], A1 + 10240)
        bias_s = at("bias_s", [P, KVH, KXW + 1], A1 + 12288)
        stat = at("stat", [P, 7, 4, 4], A1 + 13408)
        tails = at("tails", [P, PT_, PSTATE + SROWS], A1 + 13856)
        qo = at("qo", [P, 2, GRP, ROWS], R24, f32r)
        kk = at("kk", [P, 2, ROWS], R32, f32r)
        vT = at("vT", [P, ROWS], R32 + 2 * T)
        vnew = at("vnew", [T_DEC, NB_DEC, KVW], R32 + 2 * T)
        vr = at("vr", [P, NBLK, KVW], R32 + 3 * T)
        kf = at("kf", [P, WIN + SROWS], R32 + 3 * T + 4096)
        pr = at("pr", [P, 2, 4, 2 * WIN], A2)
        pt = at("pt", [P, 8, P], A2 + 8192)
        pool_s = [at(f"pool_s{i}", [P, 399], A2 + 12288 + 1600 * i) for i in range(2)]
        inv_cnt = at("inv_cnt", [P, PT_, 16], A2 + 15488)
        kxT = at("kxT", [P, NB_DEC, KXW], A3)
        qs = at("qs", [P, NB_DEC, GRP, T_DEC], A3 + 4352)
        src_s = at("src_s", [32, KVH, KXW + 1], A3 + 5376)
        perm_s = at("perm_s", [32, P], A3 + 6496)
        vecrow = at("vecrow", [62, P], A3 + 7008)
        kout = at("kout", [P, 2, KVW], A3 + 7520)
        vcache = at("vcache", [P, NB_DEC, KVW], CON + 1312)
        stout = at("stout", [P, 2, PW], CON + 1312)
        zz = at("zz", [P, 2, PT_, ROWS], R32, f32r)
        sga = at("sga", [P, ROWS], A3)
        sgp = at("sgp", [P, ROWS], A3 + T)
        mix = at("mix", [P, KD, ROWS], R16)
        hh = at("hh", [P, KD, ROWS], R16)
        wo = at("wo", [P, KD, 2, D], R24, f32r)
        xre = at("xre", [P, KD, ROWS], XN)
        xre_s = at("xre_s", [SROWS, KD, P], R24 + KD * 2 * D * 4)
        sqa = [at(f"sqa{i}", [P, 384], A3 + 1536 * i) for i in range(2)]
        ssa = at("ssa", [P, 384], A3 + 3072)
        rstd = at("rstd", [P, 384], A3 + 4608)
        sqb = [at("sqb0", [P, 384], A3 + 6144), at("sqb1", [P, 384], CON + 1312)]
        ssb = at("ssb", [P, 384], CON + 2848)
        acc = at("acc", [P, KD, ROWS], R24)
        ff = at("ff", [P, 2, FB, ROWS], R32, f32r)
        xw = at("xw", [P, 2, 2, D], XN, f32r)
        yrow = at("yrow", [P, RT, D], XN + 16384)
        sqy = [at(f"sqy{i}", [P, 512], XN + 53248 + 2048 * i) for i in range(2)]
        ssy = at("ssy", [P, 512], XN + 57344)
        rsy = at("rsy", [P, 512], XN + 59392)
        ident = at("ident", [P, P], CON)
        ones = at("ones", [P, P], CON + 512)
        vec = at("vec", [P, 64], CON + 1024)
        sink = at("sink", [P, HEADS], CON + 1280)
        V_G1, V_G2, V_G3, V_PS, V_EPS = 34, 42, 50, 58, 62
        eps = vec[:, V_EPS:V_EPS + 1]
        raw = at("raw", [P, 2, D], RING)
        wr = at("wr", [P, 2, 2, D], RING + 8192, f32r)

        ps = ctx.enter_context(nc.psum_tensor("ps", [P, 8, 512], f32))
        bias_dram = nc.dram_tensor("bias_by_distance", [HEADS, FY], f32).ap()

        def sem(name):
            return ctx.enter_context(nc.semaphore(name))

        raw_in = [sem(f"raw_in{i}") for i in range(2)]
        w_hi, w_lo, done = sem("w_hi"), sem("w_lo"), sem("group_done")
        freed = {"A": sem("freed_by_scalar"), "D": sem("freed_by_vector")}
        x_in = [sem(f"x_in{i}") for i in range(RT)]
        gbc_in, vec_in, tab_in, kc_in, st_in = (sem(n) for n in ("gbc_in", "vec_in", "tab_in", "kc_in", "st_in"))
        late_in, src_in, rev_in, brow_out = (sem(n) for n in ("late_in", "src_in", "rev_in", "brow_out"))
        eps_set, ident_set, zeroed, consts = (sem(n) for n in ("eps_set", "ident_set", "zeroed", "consts"))
        x_ss, x_sd, x_rs, x_n, x_t, x_hi, x_lo = (sem("x_" + n) for n in ("ss", "sd", "rs", "n", "t", "hi", "lo"))
        vec_t, vec_r, brow_p, brow_r = (sem(n) for n in ("vec_t", "vec_r", "brow_p", "brow_r"))
        kc_t, kc_r, st_t, st_r = (sem(n) for n in ("kc_t", "kc_r", "st_t", "st_r"))
        sb_p, bias_p, bias_r, pads = (sem(n) for n in ("sb_p", "bias_p", "bias_r", "pads"))
        v_t, v_r, vn_r, ko_r, kf_r, in_hi = (sem(n) for n in ("v_t", "v_r", "vn_r", "ko_r", "kf_r", "in_hi"))
        qk, s_free, stats, dvs, expd = (sem(n) for n in ("qk", "s_free", "stats", "dvs", "expd"))
        pt_t, pt_a, pt_d, pv = (sem(n) for n in ("pt_t", "pt_a", "pt_d", "pv"))
        o_norm, o_t, o_hi, o_lo = (sem(n) for n in ("o_norm", "o_t", "o_hi", "o_lo"))
        pl, pooled, st_o, st_or, z_hi = (sem(n) for n in ("pool_steps", "pooled", "st_o", "st_or", "z_hi"))
        mixed, m_hi, m_lo, e_sq, e_add = (sem(n) for n in ("mixed", "m_hi", "m_lo", "e_sq", "e_add"))
        n_sum, n_sd, n_rs, n_t, n_h, n_sq, n_add = (sem("n_" + n) for n in ("sum", "sd", "rs", "t", "h", "sq", "add"))
        n2_t, n2_hi, n2_lo, xr_in, xr_t = (sem(n) for n in ("n2_t", "n2_hi", "n2_lo", "xr_in", "xr_t"))
        f_sq, f_hi, f_lo = sem("f_sq"), sem("f_hi"), sem("f_lo")
        y_t, y_h, y_hp, y_p = (sem(n) for n in ("y_t", "y_h_vector", "y_h_pool", "y_p"))
        y_r = [sem(f"y_read{half}") for half in range(2)]
        y_out, moved_out, rows_out, state_out = (sem(n) for n in ("y_out", "moved_out", "rows_out", "state_out"))
        block = ctx.enter_context(nc.Block())

        def bank_of(g):
            return g % 2 if g < G_GATE0 else g % 4

        def before_in_bank(g):
            q = g - 1
            while q >= 0 and bank_of(q) != bank_of(g):
                q -= 1
            return q

        def slot(n):
            if U_E < n < U_M:
                s, i = wo, n - U_E
            elif U_M <= n < U_M + FB - 1:
                s, i = wo, n - U_M
            elif n >= N_UNITS - 2:
                s, i = xw, n % 2
            else:
                s, i = wr, n % 2
            return s[:, i, 0, :], s[:, i, 1, :]

        def slot_free(n):
            if U_E < n <= U_M:
                return G_E
            if U_M < n < U_M + FB - 1:
                return unit_end(U_E + n - U_M)
            if n == U_M + FB:
                return unit_end(U_E)
            if n == U_M + FB - 1:
                return G_E
            if n >= N_UNITS - 2:
                return unit_end(N_UNITS - 5)
            return unit_end(n - 2) if n >= 2 else 0

        def is_block(blk, n):
            return isinstance(blk, int) and blk == n

        def g_up(blk, j, c):
            if is_block(blk, 0):
                return G_M + BLOCK0.index(("up", j, c))
            return G_M + (UP_G + DOWN_G) * blk + NC_ * j + c

        def g_down(blk, m, c):
            if is_block(blk, 0):
                return G_M + BLOCK0.index(("down", m, c))
            return G_M + (UP_G + DOWN_G) * blk + UP_G + (KD * c + m if is_block(blk, LAST) else NC_ * m + c)

        def e_up(blk, j, c):
            return UP_G * blk + (FB * c + j if is_block(blk, 0) else NC_ * j + c)

        def ycs(c):
            return slice(YCH[c][0], YCH[c][0] + YCH[c][1])

        def cs(c):
            return slice(CH[c][0], CH[c][0] + CH[c][1])

        def place(m):
            return (m + KD - 2) % KD

        MAIN = [(j, c) for j in range(FB) for c in range(NC_)]
        DOWN = [(m, c) for m in range(KD) for c in range(NC_)]
        STAGE3 = [(j, c) for c in range(2) for j in range(FB)]
        EARLY = [o[1:] for o in BLOCK0[2 * FB:2 * FB + 3]]
        DOWN0 = [o[1:] for o in BLOCK0[UP_G + 3:]]
        U_LASTD = U_M + 8 * LAST + FB

        Y_AT = {(2, 2): [0], (2, 4): [1], (2, 6): [2], (2, 7): [3], (3, 1): [4], (3, 2): [5], (3, 3): [6], (3, 7): [7, 8]}
        Y_PAIR = {(1, 2): (0, 0), (1, 4): (0, 1), (1, 6): (0, 2), (2, 0): (0, 3)}
        Y_PAIR.update({(c + 1, 2 + i): (c, i) for c in (1, 2) for i in range(KD // 2)})

        def y_turned(r, half):
            return 2 * r + half + 1 if r < RT - 2 else 2 * (RT - 2) + 2 * half + (r - RT + 2) + 1

        def y_chunk(r):
            return max(c for c in range(NC_) if YCH[c][0] <= r * P)

        def bank_up(blk, j, c):
            return bank_of(g_up(blk if isinstance(blk, int) else 1, j, c))

        def bank_down(blk, m, c):
            return bank_of(g_down(blk if isinstance(blk, int) else 1, m, c))

        def vcol(n):
            return {U_K: GRP, U_V: GRP + 1}.get(n, n - U_Q if n < U_UP else n)

        MX, MM, NM, DD, ES, LL, RR = range(7)

        def keys(u, x):
            if u == A_UNITS - 1:
                return 0, KXW
            return (WIN, WIN) if u % 4 == 0 and x % 2 == 0 else (0, 2 * WIN)

        def scores(x):
            return ps[:, 2 + x // 2, (x % 2) * 2 * WIN:(x % 2 + 1) * 2 * WIN]

        def o_place(u, part, half):
            if u < A_UNITS - 1:
                c0 = (2 * (u % 4) + half) * P
                return qo[:, part, u // 4, c0:c0 + P], ps[:, 7, half * P:(half + 1) * P]
            c0 = SEQ + half * 4 * T_DEC
            dst = qo[:, part, :, c0:c0 + 4 * T_DEC].rearrange("p i (b t) -> p i b t", t=T_DEC)
            src = ps[:, 7, half * P:(half + 1) * P].rearrange("p (b i t) -> p i b t", b=4, i=GRP)
            return dst, src

        @block.sync
        def _(sp):
            def unit(n, s):
                sp.dma_start(raw[:, s, :], I["weights"][n]).then_inc(raw_in[s], 16)

            def x_load(r):
                if r < NBLK:
                    sp.dma_start(xrow[:, r, :], I["x_prompt"][0, r * P:(r + 1) * P, :]).then_inc(x_in[r], 16)
                else:
                    sp.dma_start(xrow_s[:, :], I["x_sample"].rearrange("b t n -> (b t) n")).then_inc(x_in[r], 16)

            x_load(0)
            sp.dma_start(gbc[:, :], I["norm_pre_mix"].to_broadcast([P, D])).then_inc(gbc_in, 16)
            sp.dma_start(vecrow[:, :], I["vectors"]).then_inc(vec_in, 16)
            x_load(1)
            sp.dma_start(table[:, :], I["rel_bias_table"]).then_inc(tab_in, 16)
            sp.dma_start(onehot[:, :], I["bucket_onehot"]).then_inc(tab_in, 16)
            x_load(2)
            unit(U_K, 0)
            x_load(3)
            sp.dma_start(kcache[:, :, :], I["cache_k_win"][0].rearrange("b s g d -> s b (g d)")).then_inc(kc_in, 16)
            x_load(4)
            unit(U_V, 1)
            sp.dma_start(state_in[:, :], I["state_pool"][0].rearrange("b s n -> (b s) n")).then_inc(st_in, 16)
            for r in range(5, RT):
                x_load(r)
            with sp.Fori(1, N_UNITS // 2) as pair:
                for s in range(2):
                    sp.wait_ge(w_lo, pair * 2 + (s - 1))
                    unit(pair * 2 + s, s)
            for r in range(RT):
                for half in range(2):
                    sp.wait_ge(y_r[half], r + 1)
                if r < NBLK:
                    sp.dma_start(O["y_prompt"][0, r * P:(r + 1) * P, :], yrow[:, r, :]).then_inc(y_out, 16)
                else:
                    sp.dma_start(O["y_sample"].rearrange("b t n -> (b t) n"), yrow[0:SROWS, r, :]).then_inc(y_out, 16)
            sp.wait_ge(y_out, 16 * RT)

        @block.gpsimd
        def _(pool):
            pool.memset(eps, EPS).then_inc(eps_set, 1)
            pool.memset(ident[:, :], 0.0).then_inc(zeroed, 1)
            pool.wait_ge(zeroed, 1)
            pool.affine_select(out=ident[:, :], in_=ident[:, :], compare_op=ALU.not_equal, fill=1.0,
                               base=0, pattern=[[-1, P]], channel_multiplier=1).then_inc(ident_set, 1)
            pool.memset(brow[:, :], NEG).then_inc(consts, 1)
            pool.memset(anti[:, :], 0.0).then_inc(zeroed, 1)
            pool.memset(ones[:, :], 1.0).then_inc(consts, 1)
            pool.wait_ge(zeroed, 2)
            pool.affine_select(out=anti[:, :], in_=anti[:, :], compare_op=ALU.not_equal, fill=1.0,
                               base=1 - P, pattern=[[1, P]], channel_multiplier=1).then_inc(consts, 1)
            pool.dma_start(vcache[:, :, :], I["cache_v_win"][0].rearrange("b s g d -> s b (g d)")).then_inc(late_in, 16)
            pool.dma_start(sink[:, :], I["attn_sinks"].to_broadcast([P, HEADS])).then_inc(src_in, 16)
            pool.dma_start(perm_s[:, :], I["query_perm"]).then_inc(src_in, 16)
            pool.dma_start(src_s[:, :, KXW:KXW + 1], I["sink_rows"].unsqueeze(2), allow_slow_non_contiguous=True)\
                .then_inc(src_in, 16)
            pool.wait_ge(brow_r, 1)
            pool.dma_start(bias_dram, brow[:, :]).then_inc(brow_out, 16)
            pool.wait_ge(brow_out, 16)
            pool.dma_start(bias_rev[:, :, :], bass.AP(tensor=bias_dram.tensor, offset=0,
                           ap=[[1, P], [FY, HEADS], [1, 2 * WIN]])).then_inc(rev_in, 16)
            for i in range(GRP):
                pool.dma_start(src_s[T_DEC * i:T_DEC * (i + 1), :, 0:KXW], bass.AP(
                    tensor=bias_dram.tensor, offset=FY * i + WIN - T_DEC,
                    ap=[[1, T_DEC], [FY * GRP, KVH], [1, KXW]])).then_inc(src_in, 16)
            pool.dma_start(wgrp[:, :, :], I["w_pool_grp"][0].rearrange("t c d -> c t d")).then_inc(late_in, 16)
            pool.dma_start(inv_cnt[:, :, :].rearrange("p t n -> p (t n)"),
                           I["inv_count"].to_broadcast([P, PT_ * 16])).then_inc(late_in, 16)
            for src, dst in (("cache_k_win", "k_win_sample"), ("cache_v_win", "v_win_sample")):
                pool.dma_start(O[dst][0, :, 0:WIN - T_DEC].rearrange("b s g d -> b (s g d)"),
                               I[src][0, :, T_DEC:WIN].rearrange("b s g d -> b (s g d)")).then_inc(moved_out, 16)
            pool.dma_start(O["pool_state_sample"][0, :, 0:PSTATE - T_DEC].rearrange("b s n -> b (s n)"),
                           I["state_pool"][0, :, T_DEC:PSTATE].rearrange("b s n -> b (s n)")).then_inc(moved_out, 16)
            pool.wait_ge(bias_p, 1)
            pool.wait_ge(kc_t, 1)
            pool.wait_ge(st_t, 1)
            pool.memset(upp[:, :, 0:PSTATE], 0.0).then_inc(pads, 1)
            pool.wait_ge(ko_r, 2)
            pool.dma_start(O["k_win_prompt"][0, 0].rearrange("s g d -> s (g d)"), kout[:, 0, :]).then_inc(rows_out, 16)
            pool.dma_start(O["k_win_sample"][0, :, WIN - T_DEC:WIN].rearrange("b t g d -> b t (g d)"),
                           kout[0:SROWS, 1, :]).then_inc(rows_out, 16)
            pool.wait_ge(v_r, 1)
            pool.dma_start(O["v_win_prompt"][0, 0].rearrange("s g d -> s (g d)"), vr[:, NBLK - 1, :]).then_inc(rows_out, 16)
            pool.wait_ge(vn_r, 1)
            pool.dma_start(O["v_win_sample"][0, :, WIN - T_DEC:WIN].rearrange("b t g d -> t b (g d)"),
                           vnew[:, :, :]).then_inc(rows_out, 16)

            steps = [0]

            def chained(ins):
                steps[0] += 1
                ins.then_inc(pl, 1)
                pool.wait_ge(pl, steps[0])

            def window(src, scratch, w, width, at_col):
                span, cur, n, i = 1, src, width + w - 1, 0
                base = at_col - (w - 1)
                while span < w:
                    n -= span
                    chained(pool.tensor_tensor(scratch[i % 2](0, n), cur(base + span, n), cur(base, n), ALU.add))
                    cur, base, span, i = scratch[i % 2], 0, 2 * span, i + 1
                return cur

            pool.wait_ge(late_in, 16 * 3)
            pool.wait_ge(pads, 1)
            EXT = PSTATE + T_DEC
            row = [lambda a, n, q=pool_s[i]: q[:, a:a + n] for i in range(2)]
            per_seq = [lambda a, n, q=pool_s[i]: q[:, 0:NB_DEC * EXT].rearrange("p (b s) -> p b s", s=EXT)[:, :, a:a + n]
                       for i in range(2)]
            for t in range(PT_):
                w = 2 ** (t + 1)
                for c, (c0, width) in enumerate(CH):
                    width = min(width, SEQ - c0)
                    pool.wait_ge(freed["A"], FREED[g_in(U_UP + t, c)][1])
                    s = window(lambda a, n: upp[:, t, a:a + n], row, w, width, PSTATE + c0)
                    first = 16 if c0 == 0 else 0
                    if first:
                        chained(pool.tensor_tensor(s(0, first), s(0, first), inv_cnt[:, t, :], ALU.mult))
                    chained(pool.tensor_scalar(s(first, width - first), s(first, width - first), 1.0 / w, None, ALU.mult))
                    chained(pool.tensor_tensor(upp[:, t, c0:c0 + width], s(0, width),
                                               upp[:, t, PSTATE + c0:PSTATE + c0 + width], ALU.subtract))
                chained(pool.tensor_copy(tails[:, t, 0:PSTATE], upp[:, t, SEQ:SEQ + PSTATE]))
                chained(pool.tensor_copy(tails[:, t, PSTATE:].rearrange("p (b s) -> p b s", s=T_DEC),
                                         ups[:, t, :, PSTATE:]))
                s = window(lambda a, n: ups[:, t, :, a:a + n], per_seq, w, T_DEC, PSTATE)
                chained(pool.tensor_scalar(s(0, T_DEC), s(0, T_DEC), 1.0 / w, None, ALU.mult))
                x = ups[:, t, :, PSTATE:]
                chained(pool.tensor_tensor(x, s(0, T_DEC), x, ALU.subtract))
                pool.sem_inc(pooled, 1)
            pool.wait_ge(st_or, 2)
            pool.dma_start(O["pool_state_prompt"][0, 0], stout[0:PSTATE, 0, :]).then_inc(state_out, 16)
            pool.dma_start(O["pool_state_sample"][0, :, PSTATE - T_DEC:PSTATE],
                           stout[0:SROWS, 1, :]).then_inc(state_out, 16)

            def add_product_squares(c, m):
                if m:
                    pool.wait_ge(e_sq, KD * c + m + 1)
                    if m > 1:
                        pool.wait_ge(e_add, 7 * c + m - 1)
                    total, square, w = (ssa, sqa, CH[c][1]) if c < NC_ else (ssy, sqy, YCH[c - NC_][1])
                    pool.tensor_tensor(total[:, 0:w], total[:, 0:w], square[m % 2][:, 0:w], ALU.add).then_inc(e_add, 1)

            def add_h_squares(c, k):
                if k:
                    pool.wait_ge(n_sq, KD * c + k + 1)
                    if k > 1:
                        pool.wait_ge(n_add, 7 * c + k - 1)
                    w = CH[c][1]
                    pool.tensor_tensor(ssb[:, 0:w], ssb[:, 0:w], sqb[k % 2][:, 0:w], ALU.add).then_inc(n_add, 1)

            for st in range(NC_ + 1):
                for m in range(KD):
                    if st < NC_:
                        add_product_squares(st, m)
                    if st and 1 <= m <= 4:
                        add_h_squares(st - 1, 2 * m - 2)
                        add_h_squares(st - 1, 2 * m - 1)
            for st in range(NC_ + 1):
                for m in range(KD):
                    if st < NC_:
                        add_product_squares(NC_ + st, m)
                    if (st, m) in Y_PAIR:
                        c, i = Y_PAIR[st, m]
                        k = 2 * i + 1
                        pool.wait_ge(y_t, KD * c + k)
                        pool.tensor_tensor(hh[:, k, ycs(c)], hh[:, k, ycs(c)], acc[:, place(k), ycs(c)], ALU.add)\
                            .then_inc(y_hp, 1)
            pool.wait_ge(moved_out, 16 * 3)
            pool.wait_ge(rows_out, 16 * 4)
            pool.wait_ge(state_out, 16 * 2)

        @block.scalar
        def _(act):
            def split(n):
                act.wait_ge(raw_in[n % 2], 16 * (n // 2 + 1))
                if slot_free(n):
                    act.wait_ge(done, slot_free(n))
                act.activation(slot(n)[0], raw[:, n % 2, :], ACT.Copy).then_inc(w_hi, 1)

            def x_stats(r):
                n = P if r < NBLK else SROWS
                src = xrow[:, r, :] if r < NBLK else xrow_s[:, :]
                act.wait_ge(x_in[r], 16)
                act.wait_ge(x_sd, r + 1)
                act.activation(xsq[0:n, :], src, ACT.Square, accum_out=ss[0:n, r:r + 1]).then_inc(x_ss, 1)
                act.wait_ge(x_ss, r + 1)
                act.activation(rs[0:n, r:r + 1], ss[0:n, r:r + 1], ACT.Sqrt, bias=eps[0:n], scale=1.0 / D).then_inc(x_sd, 1)

            def x_high(r):
                n = P if r < NBLK else SROWS
                act.wait_ge(x_t, r + 1)
                src = ps[:, 2 + 2 * (r % 2):4 + 2 * (r % 2), :].rearrange("p a (k n) -> p (a k) n", n=P)
                act.activation(xn[:, 0, :, r * P:r * P + n], src[:, :, 0:n], ACT.Copy).then_inc(x_hi, 1)

            def in_group(n, c):
                g = g_in(n, c)
                c0, w = CH[c]
                b = vec[:, vcol(n):vcol(n) + 1]
                act.wait_ge(done, g + 1)
                src = ps[:, bank_of(g), 0:w]
                if n == U_V:
                    act.activation(vT[:, cs(c)], src, ACT.Identity, bias=b).then_inc(freed["A"], 1)
                elif n >= U_UP:
                    t = n - U_UP
                    np_ = min(w, SEQ - c0)
                    one = act.activation(upp[:, t, PSTATE + c0:PSTATE + c0 + np_], src[:, 0:np_], ACT.Identity, bias=b)
                    if w > np_:
                        one = act.activation(ups[:, t, :, PSTATE:],
                                             src[:, np_:w].rearrange("p (b s) -> p b s", s=T_DEC), ACT.Identity, bias=b)
                    one.then_inc(freed["A"], 1)
                else:
                    dst = kk[:, 0, cs(c)] if n == U_K else qo[:, 0, n - U_Q, cs(c)]
                    act.activation(dst, src, ACT.Identity, bias=b).then_inc(in_hi, 1)

            act.wait_ge(eps_set, 1)
            act.activation(rs[:, 0:1], eps, ACT.Sqrt).then_inc(x_sd, 1)
            act.wait_ge(x_sd, 1)
            x_stats(0)
            x_stats(1)
            x_high(0)
            x_stats(2)
            split(U_K)
            x_high(1)
            x_stats(3)
            x_high(2)
            split(U_V)
            x_stats(4)
            x_stats(5)
            act.wait_ge(kc_t, 1)
            act.activation(kxT[:, :, 0:WIN], ps[:, 6:8, :].rearrange("p a (b n) -> p (a b) n", n=P), ACT.Copy)\
                .then_inc(kc_r, 1)
            x_high(3)
            x_stats(6)
            x_high(4)
            act.wait_ge(vec_r, 1)
            in_group(U_K, 0)
            x_high(5)
            x_stats(7)
            in_group(U_V, 0)
            x_high(6)
            x_stats(8)
            x_high(7)
            in_group(U_K, 1)
            x_high(8)
            in_group(U_V, 1)
            in_group(U_K, 2)
            split(U_Q)
            in_group(U_V, 2)
            in_group(U_Q, 0)
            split(U_Q + 1)
            act.wait_ge(v_t, 1)
            act.activation(vnew[:, :, :], ps[0:T_DEC, 6:8, :].rearrange("p a (b n) -> p (a b) n", n=P), ACT.Copy)\
                .then_inc(vn_r, 1)
            act.activation(kout[:, 0, :], ps[:, 4, 0:P], ACT.Copy).then_inc(ko_r, 1)
            act.activation(kout[0:SROWS, 1, :], ps[0:SROWS, 4, P:2 * P], ACT.Copy).then_inc(ko_r, 1)
            in_group(U_Q, 1)
            act.wait_ge(bias_p, 1)
            act.activation(bias[:, :, :], ps[:, 4:8, :].rearrange("p a (b n) -> p (a b) n", n=2 * WIN), ACT.Copy)\
                .then_inc(bias_r, 1)
            in_group(U_Q, 2)

            in_group(*filler(0))
            split(U_Q + 2)
            for s in range(A_STEPS):
                u = s - 3
                if 0 <= u < A_UNITS:
                    act.wait_ge(o_t, u + 1)
                    for half in range(2):
                        dst, src = o_place(u, 0, half)
                        act.activation(dst, src, ACT.Copy).then_inc(o_hi, 1)
                u = s
                if u < A_UNITS:
                    act.wait_ge(stats, u + 1)
                    act.activation(stat[:, ES, u % 4, :], stat[:, DD, u % 4, :], ACT.Exp, scale=SCALE)
                    for x in range(4):
                        k0, kw = keys(u, x)
                        p_ = pr[:, u % 2, x, k0:k0 + kw]
                        one = act.activation(p_, p_, ACT.Exp, bias=stat[:, NM, u % 4, x:x + 1], scale=SCALE,
                                             accum_out=stat[:, LL, u % 4, x:x + 1])
                    one.then_inc(expd, 1)
                u = s - 1
                if 0 <= u < A_UNITS:
                    act.wait_ge(pt_t, u + 1)
                    if u:
                        act.wait_ge(pv, u)
                    act.activation(pt[:, 0:4, :], ps[:, 4, :].rearrange("p (b n) -> p b n", n=P), ACT.Copy).then_inc(pt_a, 1)
                if s + 1 < FILL:
                    n, c = filler(s + 1)
                    if n == U_UP and c == 0:
                        act.wait_ge(pads, 1)
                    in_group(n, c)
                    if c == 0:
                        split(n + 1)

            def gate(j, x, c):
                g = g_gate(j, x, c)
                act.wait_ge(done, g + 1)
                if j:
                    act.wait_ge(mixed, 3 * (j - 1) + c + 1)
                act.activation((sga, sgp)[x][:, cs(c)], ps[:, bank_of(g), 0:CH[c][1]], ACT.Sigmoid,
                               bias=vec[:, 10 + KD * x + j:11 + KD * x + j]).then_inc(freed["A"], 1)
                if c == 0:
                    split(U_D + 3 * j + x + 1)

            act.wait_ge(rows_out, 16 * 4)
            for x in range(2):
                for c in range(NC_):
                    gate(0, x, c)

            act.wait_ge(st_o, 1)
            act.activation(stout[0:PSTATE, 0, :], ps[0:PSTATE, 6, :], ACT.Copy).then_inc(st_or, 1)
            act.activation(stout[0:SROWS, 1, :], ps[0:SROWS, 7, :], ACT.Copy).then_inc(st_or, 1)
            for t in range(PT_):
                for c in range(NC_):
                    g = G_GRP + NC_ * t + c
                    act.wait_ge(done, g + 1)
                    act.activation(zz[:, 0, t, cs(c)], ps[:, bank_of(g), 0:CH[c][1]], ACT.Copy,
                                   scale=vec[:, V_PS + t:V_PS + t + 1]).then_inc(z_hi, 1)

            for j in range(KD):
                if j:
                    for x in range(2):
                        for c in range(NC_):
                            gate(j, x, c)
                if j + 1 < KD:
                    act.wait_ge(done, g_mix(j, 0, 1) + 1)
                    split(U_D + 3 * j + 3)
            for c in range(NC_):
                act.wait_ge(mixed, 3 * (KD - 1))
                act.activation(xn[:, 0, 0:KD - 1, cs(c)], mix[:, 0:KD - 1, cs(c)], ACT.Copy).then_inc(m_hi, 1)
                if c == 0:
                    split(U_E)
                if c == 1:
                    split(U_E + 1)
                act.wait_ge(mixed, 3 * (KD - 1) + c + 1)
                act.activation(xn[:, 0, KD - 1, cs(c)], mix[:, KD - 1, cs(c)], ACT.Copy).then_inc(m_hi, 1)

            def product_square(c, m, src):
                total, square, w = (ssa, sqa, CH[c][1]) if c < NC_ else (ssy, sqy, YCH[c - NC_][1])
                if m == 0 and c:
                    act.wait_ge(n_sum, 2 * c - 1 if c <= NC_ else NC_ + c)
                if m >= 3:
                    act.wait_ge(e_add, 7 * c + m - 2)
                dst = total if m == 0 else square[m % 2]
                act.activation(dst[:, 0:w], src, ACT.Square).then_inc(e_sq, 1)

            def root(s, w, dst=rstd):
                act.wait_ge(n_sum, s + 1)
                act.activation(dst[:, 0:w], ps[:, 4, 0:w], ACT.Sqrt, bias=eps, scale=1.0 / D).then_inc(n_sd, 1)

            def norm_part(c, m):
                w = CH[c][1]
                if m == 0:
                    root(2 * c, w)
                elif m <= 4:
                    for k in (2 * m - 2, 2 * m - 1):
                        act.wait_ge(n_h, KD * c + k + 1)
                        if k == 0 and c == 0:
                            act.wait_ge(state_out, 16 * 2)
                        if k == 0 and c:
                            act.wait_ge(n2_lo, KD * c)
                        if k >= 3:
                            act.wait_ge(n_add, 7 * c + k - 2)
                        act.activation((ssb if k == 0 else sqb[k % 2])[:, 0:w], hh[:, k, cs(c)], ACT.Square).then_inc(n_sq, 1)
                elif m == 5:
                    root(2 * c + 1, w)
                else:
                    for k in range(4 * (m - 6), 4 * (m - 5)):
                        act.wait_ge(n2_t, KD * c + k + 1)
                        act.activation(xn[:, 0, k, cs(c)], sqb[k % 2][:, 0:w], ACT.Copy).then_inc(n2_hi, 1)

            def hidden(blk, j, c):
                g, e, w = g_up(blk, j, c), e_up(blk, j, c), CH[c][1]
                f = sqa[(NC_ * j + c if not isinstance(blk, int) else e) % 2][:, 0:w]
                act.wait_ge(done, g + 1)
                if isinstance(blk, int) and e < 2:
                    act.wait_ge(e_add, 7 * NC_)
                else:
                    act.wait_ge(f_lo, e - 1)
                act.activation(f, ps[:, bank_up(blk, j, c), 0:w], ACT.Relu).then_inc(freed["A"], 1)
                act.wait_ge(freed["A"], per_block(lambda b: FREED[g_up(b, j, c)][1], blk))
                act.activation(f, f, ACT.Square).then_inc(f_sq, 1)
                act.wait_ge(f_sq, e + 1)
                act.activation(ff[:, 0, j, cs(c)], f, ACT.Copy).then_inc(f_hi, 1)

            def split_mlp(blk, x):
                n = U_M + x
                act.wait_ge(raw_in[n % 2], per_block(lambda b: 16 * ((U_M + 8 * b + x) // 2 + 1), blk))
                act.wait_ge(done, per_block(lambda b: unit_end(U_M + 8 * b + x - 2), blk))
                act.activation(wr[:, n % 2, 0, :], raw[:, n % 2, :], ACT.Copy).then_inc(w_hi, 1)

            def x_rows(c):
                c0, w = CH[c]
                act.wait_ge(done, G_E + KD * (c + 1))
                for r in range((w + P - 1) // P):
                    n = min(P, w - r * P)
                    src = I["x_prompt"][0, c0 + r * P:c0 + r * P + P, :] if c0 + r * P < SEQ \
                        else I["x_sample"].rearrange("b t n -> (b t) n")
                    act.dma_start(xre[0:n, :, c0 + r * P:c0 + r * P + P] if n == P else xre_s[:, :, :],
                                  src.rearrange("p (k n) -> p k n", n=P)).then_inc(xr_in, 16)

            for st in range(NC_ + 1):
                for m in range(KD):
                    if st < NC_:
                        g = G_E + KD * st + m
                        act.wait_ge(done, g + 1)
                        product_square(st, m, ps[:, bank_of(g), 0:CH[st][1]])
                        act.activation(hh[:, m, cs(st)], ps[:, bank_of(g), 0:CH[st][1]], ACT.Copy).then_inc(freed["A"], 1)
                        if m == KD - 1:
                            x_rows(st)
                    else:
                        if m in (5, 6):
                            norm_part(st - 1, m)
                        hidden(0, *STAGE3[m])
                    if st == 0 and m < 6:
                        split(U_E + 2 + m)
                    if st == 2 and 2 <= m < 2 + FB:
                        split(U_M + m - 2)
                    if st == 3 and m == 2:
                        split(U_M + FB)
                    if st and not (st == NC_ and m in (5, 6)):
                        norm_part(st - 1, m)
            for j in range(FB):
                hidden(0, j, 2)
            split(U_M + FB + 1)
            for x in (6, 7, 8):
                act.wait_ge(done, g_down(0, 2 * (x - 5), 0) + 1)
                split_mlp(0, x) if x < 8 else split_mlp(1, 0)

            def mlp_block(blk):
                for j, c in MAIN:
                    hidden(blk, j, c)
                    if c == 0:
                        split_mlp(blk, j + 1)
                for x in (5, 6, 7, 8):
                    act.wait_ge(done, per_block(lambda b: G_M + (UP_G + DOWN_G) * b + UP_G + 6 * (x - 5) + 1, blk))
                    split_mlp(blk, x) if x < 8 else split_mlp(blk + 1, 0)

            with act.Fori(1, LAST) as blk:
                mlp_block(blk)
            for j, c in MAIN:
                hidden(LAST, j, c)
                if c == 0:
                    split(U_M + 8 * LAST + j + 1)

            def y_part(c, m):
                if m == 1:
                    if c:
                        act.wait_ge(y_t, KD * c)
                    root(2 * NC_ + c, YCH[c][1], rsy)
                tiles = Y_AT.get((c + 1, m), [])
                for half in range(2):
                    for r in tiles:
                        if half and r >= RT - 2:
                            continue
                        n = min(P, ROWS - r * P)
                        act.wait_ge(y_p, y_turned(r, half))
                        act.activation(yrow[0:n, r, half * 512:(half + 1) * 512], ps[0:n, 4 + 2 * (r % 2) + half, :],
                                       ACT.Copy).then_inc(y_r[half], 1)

            split(U_LASTD + 1)
            for st in range(NC_ + 1):
                for m in range(KD):
                    if st < NC_:
                        g = g_down(LAST, m, st)
                        act.wait_ge(freed["D"], FREED[g][1])
                        product_square(NC_ + st, m, acc[:, place(m), ycs(st)])
                    if st == 0 and m in (0, 1):
                        split(U_LASTD + 2 + m)
                    if st:
                        y_part(st - 1, m)

        @block.vector
        def _(dve):
            def lo(n):
                dve.wait_ge(w_hi, n + 1)
                hi_, lo_ = slot(n)
                dve.tensor_tensor(lo_, raw[:, n % 2, :], hi_.bitcast(f32), ALU.subtract).then_inc(w_lo, 1)

            steps = [0]

            def chained(ins):
                steps[0] += 1
                ins.then_inc(dvs, 1)
                dve.wait_ge(dvs, steps[0])

            def x_scale(r):
                n = P if r < NBLK else SROWS
                x = xrow[:, r, :] if r < NBLK else xrow_s[:, :]
                dve.wait_ge(x_sd, r + 2)
                dve.reciprocal(rs[0:n, r:r + 1], rs[0:n, r:r + 1]).then_inc(x_rs, 1)
                dve.wait_ge(x_rs, r + 1)
                dve.scalar_tensor_tensor(out=x, in0=x, scalar=rs[0:n, r:r + 1], in1=gbc[0:n, :],
                                         op0=ALU.mult, op1=ALU.mult).then_inc(x_n, 1)

            def x_low(r):
                n = P if r < NBLK else SROWS
                dve.wait_ge(x_hi, r + 1)
                src = ps[:, 2 + 2 * (r % 2):4 + 2 * (r % 2), :].rearrange("p a (k n) -> p (a k) n", n=P)
                dve.tensor_tensor(xn[:, 1, :, r * P:r * P + n], src[:, :, 0:n],
                                  xn[:, 0, :, r * P:r * P + n].bitcast(f32), ALU.subtract).then_inc(x_lo, 1)

            his = [0]

            def in_group(n, c):
                g = g_in(n, c)
                w = CH[c][1]
                b = vec[:, vcol(n):vcol(n) + 1]
                if n == U_V or n >= U_UP:
                    return
                his[0] += 1
                dve.wait_ge(in_hi, his[0])
                src = ps[:, bank_of(g), 0:w]
                dst = kk if n == U_K else qo[:, :, n - U_Q, :]
                if c == NC_ - 1:
                    new = src[:, w - SROWS:w]
                    if n == U_K:
                        dve.tensor_scalar(kf[:, :], src[:, w - SROWS - WIN:w], b, None, ALU.add).then_inc(kf_r, 1)
                        dve.wait_ge(kc_r, 1)
                        dve.tensor_scalar(kxT[:, :, WIN:], new.rearrange("p (b s) -> p b s", s=T_DEC), b, None, ALU.add)
                    else:
                        dve.tensor_scalar(qs[:, :, n - U_Q, :], new.rearrange("p (b s) -> p b s", s=T_DEC), b, None, ALU.add)
                dve.scalar_tensor_tensor(out=dst[:, 1, cs(c)], in0=src, scalar=b, in1=dst[:, 0, cs(c)].bitcast(f32),
                                         op0=ALU.add, op1=ALU.subtract).then_inc(freed["D"], 1)

            dve.wait_ge(gbc_in, 16)
            x_scale(0)
            x_scale(1)
            x_low(0)
            dve.wait_ge(vec_t, 1)
            dve.tensor_copy(vec[:, 0:62], ps[:, 6, 0:62]).then_inc(vec_r, 1)
            x_scale(2)
            lo(U_K)
            dve.wait_ge(brow_p, 1)
            dve.wait_ge(consts, 1)
            dve.tensor_scalar(brow[:, WIN:2 * WIN], ps[0:HEADS, 7, 0:P], 1.0 / SCALE, None, ALU.mult).then_inc(brow_r, 1)
            x_low(1)
            x_low(2)
            x_scale(3)
            lo(U_V)
            x_scale(4)
            x_scale(5)
            x_low(3)
            x_scale(6)
            x_low(4)
            in_group(U_K, 0)
            dve.wait_ge(st_t, 1)
            dve.tensor_copy(ups[:, :, :, 0:PSTATE],
                            ps[:, 6, 0:PT_ * NB_DEC * PSTATE].rearrange("p (t b s) -> p t b s", t=PT_, b=NB_DEC))\
                .then_inc(st_r, 1)
            x_low(5)
            x_scale(7)
            x_low(6)
            x_scale(8)
            x_low(7)
            in_group(U_K, 1)
            x_low(8)
            in_group(U_K, 2)
            lo(U_Q)
            in_group(U_Q, 0)
            lo(U_Q + 1)
            dve.wait_ge(v_t, 1)
            dve.tensor_copy(vr[:, :, :], ps[:, 2:4, :].rearrange("p a (b n) -> p (a b) n", n=P)).then_inc(v_r, 1)
            in_group(U_Q, 1)
            dve.wait_ge(sb_p, 1)
            chained(dve.tensor_copy(bias_s[:, :, :], ps[:, 3, 0:KVH * (KXW + 1)].rearrange("p (g n) -> p g n", g=KVH)))
            dve.tensor_scalar(bias_s[:, :, KXW:], bias_s[:, :, KXW:], 1.0 / SCALE, None, ALU.mult)
            chained(dve.tensor_scalar(sink[:, :], sink[:, :], 1.0 / SCALE, None, ALU.mult))
            in_group(U_Q, 2)

            in_group(*filler(0))
            lo(U_Q + 2)
            for s in range(A_STEPS):
                u = s
                if u < A_UNITS:
                    if u == 0:
                        dve.wait_ge(bias_r, 1)
                    dve.wait_ge(qk, u + 1)
                    if u >= 2:
                        dve.wait_ge(pt_t, u - 1)
                    for x in range(4):
                        k0, kw = keys(u, x)
                        bi = bias_s[:, x // 2, 0:KXW] if u == A_UNITS - 1 else bias[:, GRP * (x // 2) + u // 4, k0:k0 + kw]
                        one = dve.tensor_tensor_reduce(out=pr[:, u % 2, x, k0:k0 + kw], in0=scores(x)[:, k0:k0 + kw],
                                                       in1=bi, scale=1.0, scalar=-3e38, op0=ALU.add, op1=ALU.max,
                                                       accum_out=stat[:, MX, u % 4, x:x + 1])
                    one.then_inc(s_free, 1)
                    dve.wait_ge(s_free, u + 1)
                    if u < A_UNITS - 1:
                        sk = sink[:, :].rearrange("p (g i) -> p g i", g=KVH)[:, :, u // 4:u // 4 + 1].to_broadcast([P, KVH, 2])
                    else:
                        sk = bias_s[:, :, KXW:].to_broadcast([P, KVH, 2])
                    v4 = lambda row: stat[:, row, u % 4, :].rearrange("p (g b) -> p g b", g=KVH)
                    chained(dve.tensor_tensor(v4(MM), v4(MX), sk, ALU.max))
                    dve.tensor_tensor(v4(DD), sk, v4(MM), ALU.subtract)
                    dve.tensor_scalar(stat[:, NM, u % 4, :], stat[:, MM, u % 4, :], -SCALE, None, ALU.mult).then_inc(stats, 1)
                u = s - 2
                if 0 <= u < A_UNITS:
                    dve.wait_ge(expd, u + 1)
                    chained(dve.tensor_tensor(stat[:, RR, u % 4, :], stat[:, LL, u % 4, :], stat[:, ES, u % 4, :], ALU.add))
                    chained(dve.reciprocal(stat[:, RR, u % 4, :], stat[:, RR, u % 4, :]))
                    dve.wait_ge(pv, u + 1)
                    if u:
                        dve.wait_ge(o_t, u)
                    dve.tensor_tensor(orow[:, :, :, :].rearrange("p b g d -> p g b d"),
                                      ps[:, 6, 0:4 * HD].rearrange("p (g b d) -> p g b d", g=KVH, d=HD),
                                      stat[:, RR, u % 4, :].rearrange("p (g b) -> p g b", g=KVH).unsqueeze(3)
                                      .to_broadcast([P, KVH, 2, HD]), ALU.mult).then_inc(o_norm, 1)
                u = s - 3
                if 0 <= u < A_UNITS:
                    dve.wait_ge(o_hi, 2 * u + 2)
                    for half in range(2):
                        dst, src = o_place(u, 1, half)
                        dve.tensor_tensor(dst, src, o_place(u, 0, half)[0].bitcast(f32), ALU.subtract).then_inc(o_lo, 1)
                u = s - 1
                if 0 <= u < A_UNITS:
                    dve.wait_ge(pt_t, u + 1)
                    if u:
                        dve.wait_ge(pv, u)
                    dve.tensor_copy(pt[:, 4:8, :], ps[:, 5, :].rearrange("p (b n) -> p b n", n=P)).then_inc(pt_d, 1)
                if s + 1 < FILL:
                    n, c = filler(s + 1)
                    in_group(n, c)
                    if c == 0:
                        lo(n + 1)
            lo(U_D + 1)
            lo(U_D + 2)

            for t in range(PT_):
                for c in range(NC_):
                    g = G_GRP + NC_ * t + c
                    dve.wait_ge(z_hi, NC_ * t + c + 1)
                    dve.scalar_tensor_tensor(out=zz[:, 1, t, cs(c)], in0=ps[:, bank_of(g), 0:CH[c][1]],
                                             scalar=vec[:, V_PS + t:V_PS + t + 1], in1=zz[:, 0, t, cs(c)].bitcast(f32),
                                             op0=ALU.mult, op1=ALU.subtract).then_inc(freed["D"], 1)

            def mix_part(j, c, x):
                w, g = CH[c][1], g_mix(j, c, x)
                gate = (sga, sgp)[x][:, cs(c)]
                dve.wait_ge(done, g + 1)
                dve.wait_ge(freed["A"], FREED[g_gate(j, x, c)][1])
                dve.tensor_tensor(gate, ps[:, bank_of(g), 0:w], gate, ALU.mult).then_inc(freed["D"], 1)
                if x:
                    dve.wait_ge(freed["D"], FREED[g][1])
                    dve.tensor_tensor(mix[:, j, cs(c)], sga[:, cs(c)], gate, ALU.add).then_inc(mixed, 1)

            def mix_low(c, last):
                k0, k1 = (KD - 1, KD) if last else (0, KD - 1)
                dve.wait_ge(m_hi, 2 * c + last + 1)
                dve.tensor_tensor(xn[:, 1, k0:k1, cs(c)], mix[:, k0:k1, cs(c)], xn[:, 0, k0:k1, cs(c)].bitcast(f32),
                                  ALU.subtract).then_inc(m_lo, 1)

            for j in range(KD):
                n = U_D + 3 * j
                if j:
                    lo(n + 1)
                    lo(n + 2)
                for c, x in mix_order(j):
                    mix_part(j, c, x)
                    if (c, x) == (0, 1) and j + 1 < KD:
                        lo(n + 3)
                    if (c, x) == (0, 1) and j == KD - 1:
                        mix_low(0, 0)
                        lo(U_E)
                        mix_low(0, 1)
            lo(U_E + 1)

            def invert(s, w, r=rstd):
                dve.wait_ge(n_sd, s + 1)
                dve.reciprocal(r[:, 0:w], r[:, 0:w]).then_inc(n_rs, 1)
                dve.wait_ge(n_rs, s + 1)

            def norm_part(c, m):
                w = CH[c][1]
                if m == 0:
                    invert(2 * c, w)
                elif m <= 4:
                    for k in (2 * m - 2, 2 * m - 1):
                        h = hh[:, k, cs(c)]
                        dve.scalar_tensor_tensor(out=h, in0=h, scalar=vec[:, V_G1 + k:V_G1 + k + 1], in1=rstd[:, 0:w],
                                                 op0=ALU.mult, op1=ALU.mult).then_inc(n_t, 1)
                    for k in (2 * m - 2, 2 * m - 1):
                        h = hh[:, k, cs(c)]
                        dve.wait_ge(n_t, KD * c + k + 1)
                        dve.wait_ge(xr_t, KD * c + k + 1)
                        dve.tensor_tensor(h, h, ps[:, 5 + k % 2, 0:w], ALU.add).then_inc(n_h, 1)
                elif m == 5:
                    invert(2 * c + 1, w)
                else:
                    for k0 in (4 * (m - 6), 4 * (m - 6) + 2):
                        for k in (k0, k0 + 1):
                            if k >= 2:
                                dve.wait_ge(n2_lo, KD * c + k - 1)
                            dve.scalar_tensor_tensor(out=sqb[k % 2][:, 0:w], in0=hh[:, k, cs(c)],
                                                     scalar=vec[:, V_G2 + k:V_G2 + k + 1], in1=rstd[:, 0:w],
                                                     op0=ALU.mult, op1=ALU.mult).then_inc(n2_t, 1)
                        for k in (k0, k0 + 1):
                            dve.wait_ge(n2_hi, KD * c + k + 1)
                            dve.tensor_tensor(xn[:, 1, k, cs(c)], sqb[k % 2][:, 0:w], xn[:, 0, k, cs(c)].bitcast(f32),
                                              ALU.subtract).then_inc(n2_lo, 1)

            def hidden_low(blk, j, c):
                e, w = e_up(blk, j, c), CH[c][1]
                f = sqa[(NC_ * j + c if not isinstance(blk, int) else e) % 2][:, 0:w]
                dve.wait_ge(f_hi, e + 1)
                dve.tensor_tensor(ff[:, 1, j, cs(c)], f, ff[:, 0, j, cs(c)].bitcast(f32), ALU.subtract).then_inc(f_lo, 1)

            def lo_mlp(blk, x):
                n = U_M + x
                dve.wait_ge(w_hi, blk * 8 + (n + 1))
                dve.tensor_tensor(wr[:, n % 2, 1, :], raw[:, n % 2, :], wr[:, n % 2, 0, :].bitcast(f32), ALU.subtract)\
                    .then_inc(w_lo, 1)

            def gather(blk, m, c):
                g, w = g_down(blk, m, c), (YCH if is_block(blk, LAST) else CH)[c][1]
                dve.wait_ge(done, g + 1)
                src = ps[:, bank_down(blk, m, c), 0:w]
                a = acc[:, place(m), ycs(c) if is_block(blk, LAST) else cs(c)]
                if is_block(blk, 0):
                    dve.tensor_copy(a, src).then_inc(freed["D"], 1)
                else:
                    dve.tensor_tensor(a, a, src, ALU.add).then_inc(freed["D"], 1)

            for st in range(NC_ + 1):
                for m in range(KD):
                    if st and m == 0:
                        dve.wait_ge(freed["A"], FREED[G_E + KD * st - 1][1])
                    if st and not (st == NC_ and m == 7):
                        norm_part(st - 1, m)
                    if st == NC_:
                        hidden_low(0, *STAGE3[m])
                        if m == 7:
                            norm_part(st - 1, m)
                    if st == 0 and m < 6:
                        lo(U_E + 2 + m)
                    if st == 0 and m in (1, 3):
                        for last in range(2):
                            mix_low((m + 1) // 2, last)
                    if st == 2 and 2 <= m < 2 + FB:
                        lo(U_M + m - 2)
                    if st == 3 and m == 2:
                        lo(U_M + FB)
            for m, c in EARLY:
                gather(0, m, c)
            for j in range(FB):
                hidden_low(0, j, 2)
            lo(U_M + FB + 1)
            for m, c in DOWN0:
                gather(0, m, c)
                if m % 2 == 0 and m and c == 0:
                    x = FB + m // 2 + 1
                    lo_mlp(0, x) if x < 8 else lo_mlp(1, 0)

            def mlp_block(blk):
                for j, c in MAIN:
                    hidden_low(blk, j, c)
                    if c == 0:
                        lo_mlp(blk, j + 1)
                for m, c in DOWN:
                    gather(blk, m, c)
                    if m % 2 == 0 and c == 0:
                        x = FB + m // 2 + 1
                        lo_mlp(blk, x) if x < 8 else lo_mlp(blk + 1, 0)

            with dve.Fori(1, LAST) as blk:
                mlp_block(blk)
            for j, c in MAIN:
                hidden_low(LAST, j, c)
                if c == 0:
                    lo(U_M + 8 * LAST + j + 1)
            lo(U_LASTD + 1)

            def y_part(c, m):
                if m == 1:
                    invert(2 * NC_ + c, YCH[c][1], rsy)
                if (c + 1, m) in Y_PAIR:
                    c, i = Y_PAIR[c + 1, m]
                    for k in (2 * i + 1, 2 * i):
                        a = acc[:, place(k), ycs(c)]
                        one = dve.scalar_tensor_tensor(out=a, in0=a, scalar=vec[:, V_G3 + k:V_G3 + k + 1],
                                                       in1=rsy[:, 0:YCH[c][1]], op0=ALU.mult, op1=ALU.mult)
                        one.then_inc(y_t, 1)
                    dve.wait_ge(y_t, KD * c + k + 2)
                    h = hh[:, k, ycs(c)]
                    dve.tensor_tensor(h, h, acc[:, place(k), ycs(c)], ALU.add).then_inc(y_h, 1)
                if (c, m) == (NC_ - 1, 7):
                    for r in (RT - 2, RT - 1):
                        n = min(P, ROWS - r * P)
                        dve.wait_ge(y_p, y_turned(r, 1))
                        dve.wait_ge(y_r[1], r)
                        dve.tensor_copy(yrow[0:n, r, D // 2:D], ps[0:n, 5 + 2 * (r % 2), :]).then_inc(y_r[1], 1)

            for st in range(NC_ + 1):
                for m in range(KD):
                    if st < NC_:
                        gather(LAST, m, st)
                    if st == 0 and m in (0, 1):
                        lo(U_LASTD + 2 + m)
                    if st:
                        y_part(st - 1, m)

        @block.tensor
        def _(pe):
            def need(n):
                pe.wait_ge(w_lo, n + 1)

            def bank_free(g):
                q = before_in_bank(g)
                if q >= 0:
                    pe.wait_ge(freed[FREED[q][0]], FREED[q][1])

            def products(out, terms, inc):
                last = len(terms) - 1
                for i, ((wh, wl), (rh, rl)) in enumerate(terms):
                    pe.matmul(out, wh, rh, start=(i == 0), stop=False)
                    pe.matmul(out, wh, rl, start=False, stop=False)
                    mm = pe.matmul(out, wl, rh, start=False, stop=(i == last))
                if inc:
                    mm.then_inc(done, 1)

            def wtile(n, k):
                h, l = slot(n)
                return h[:, k * P:(k + 1) * P], l[:, k * P:(k + 1) * P]

            def rows(t, k, c):
                return t[:, 0, k, cs(c)], t[:, 1, k, cs(c)]

            def full_group(g, n, c):
                bank_free(g)
                products(ps[:, bank_of(g), 0:CH[c][1]], [(wtile(n, k), rows(xn, k, c)) for k in range(KD)], True)

            def turn(out, src, n=P):
                return pe.transpose(out, src, ident[0:n, 0:n])

            def x_turn(r):
                n = P if r < NBLK else SROWS
                pe.wait_ge(x_n, r + 1)
                if r >= 2:
                    pe.wait_ge(x_lo, r - 1)
                for k in range(KD):
                    src = xrow[:, r, k * P:(k + 1) * P] if r < NBLK else xrow_s[:, k * P:(k + 1) * P]
                    mm = turn(ps[:, 2 + 2 * (r % 2) + k // 4, (k % 4) * P:(k % 4) * P + n], src, n)
                mm.then_inc(x_t, 1)

            pe.wait_ge(ident_set, 1)
            x_turn(0)
            pe.wait_ge(vec_in, 16)
            turn(ps[:, 6, 0:62], vecrow[:, :], 62).then_inc(vec_t, 1)
            x_turn(1)
            pe.wait_ge(tab_in, 16 * 2)
            pe.matmul(ps[0:HEADS, 7, 0:P], table[:, :], onehot[:, :], start=True, stop=True).then_inc(brow_p, 1)
            x_turn(2)
            pe.wait_ge(vec_r, 1)
            pe.wait_ge(brow_r, 1)
            pe.wait_ge(kc_in, 16)
            for b in range(NB_DEC):
                mm = turn(ps[:, 6 + b // 4, (b % 4) * P:(b % 4 + 1) * P], kcache[:, b, :])
            mm.then_inc(kc_t, 1)

            def kv_group(n, c):
                need(n)
                pe.wait_ge(x_lo, min(3 * c + 3, RT))
                full_group(g_in(n, c), n, c)

            kv_group(U_K, 0)
            x_turn(3)
            x_turn(4)
            pe.wait_ge(kc_r, 1)
            pe.wait_ge(st_in, 16)
            for t in range(PT_):
                ns = NB_DEC * PSTATE
                mm = turn(ps[:, 6, t * ns:(t + 1) * ns], state_in[:, t * P:(t + 1) * P], ns)
            mm.then_inc(st_t, 1)
            kv_group(U_V, 0)
            x_turn(5)
            x_turn(6)
            kv_group(U_K, 1)
            x_turn(7)
            x_turn(8)
            kv_group(U_V, 1)
            kv_group(U_K, 2)
            kv_group(U_V, 2)
            need(U_Q)
            full_group(g_in(U_Q, 0), U_Q, 0)
            pe.wait_ge(freed["A"], FREED[g_in(U_V, 2)][1])
            pe.wait_ge(st_r, 1)
            pe.wait_ge(x_lo, RT)
            pe.wait_ge(kf_r, 1)
            for b in range(NBLK):
                turn(ps[:, 2 + b // 4, (b % 4) * P:(b % 4 + 1) * P], vT[:, b * P:(b + 1) * P])
            for b in range(NB_DEC):
                turn(ps[0:T_DEC, 6 + b // 4, (b % 4) * P:(b % 4 + 1) * P], vT[:, SEQ + b * T_DEC:SEQ + (b + 1) * T_DEC])
            turn(ps[:, 4, 0:P], kf[:, 0:WIN])
            turn(ps[0:SROWS, 4, P:2 * P], kf[:, WIN:]).then_inc(v_t, 1)
            full_group(g_in(U_Q, 1), U_Q, 1)
            pe.wait_ge(v_r, 1)
            pe.wait_ge(vn_r, 1)
            pe.wait_ge(ko_r, 2)
            pe.wait_ge(consts, 3)
            pe.wait_ge(rev_in, 16)
            for i in range(4):
                mm = pe.matmul(ps[:, 4 + i, :], anti[:, :], bias_rev[:, 2 * i:2 * i + 2, :], start=True, stop=True)
            mm.then_inc(bias_p, 1)
            pe.wait_ge(src_in, 16 * 7)
            pe.matmul(ps[:, 3, 0:KVH * (KXW + 1)], perm_s[:, :], src_s[:, :, :], start=True, stop=True).then_inc(sb_p, 1)
            full_group(g_in(U_Q, 2), U_Q, 2)

            def score_products(u):
                if u == 0:
                    pe.wait_ge(dvs, 2)
                if u:
                    pe.wait_ge(s_free, u)
                if u < A_UNITS - 1:
                    if u % 4 == 0:
                        pe.wait_ge(freed["D"], FREED[g_in(U_Q + u // 4, 2)][1])
                    for x in (0, 2, 1, 3):
                        g, b, (k0, kw) = x // 2, 2 * (u % 4) + x % 2, keys(u, x)
                        lane = slice(g * HD, (g + 1) * HD)
                        kc = slice((b - 1) * P + k0, (b - 1) * P + k0 + kw)
                        q_ = [qo[lane, part, u // 4, b * P:(b + 1) * P] for part in range(2)]
                        k_ = [kk[lane, part, kc] for part in range(2)]
                        out = scores(x)[:, k0:k0 + kw]
                        pe.matmul(out, q_[0], k_[0], start=True, stop=False)
                        pe.matmul(out, q_[0], k_[1], start=False, stop=False)
                        mm = pe.matmul(out, q_[1], k_[0], start=False, stop=True)
                else:
                    for b in range(NB_DEC):
                        for g in range(KVH):
                            lane, part = slice(g * HD, (g + 1) * HD), slice(32 * (b % 4), 32 * (b % 4) + 32)
                            mm = pe.matmul(scores(2 * g + b // 4)[part, 0:KXW], qs[lane, b, :, :].rearrange("p i t -> p (i t)"),
                                           kxT[lane, b, :], start=True, stop=True)
                mm.then_inc(qk, 1)

            def turn_probs(u):
                pe.wait_ge(expd, u + 1)
                if u:
                    pe.wait_ge(pt_a, u)
                    pe.wait_ge(pt_d, u)
                else:
                    pe.wait_ge(bias_r, 1)
                for x in range(4):
                    k0, kw = keys(u, x)
                    for h in range(2):
                        a, n = h * WIN, min(WIN, k0 + kw - h * WIN)
                        if a < k0:
                            a = WIN
                        mm = turn(ps[0:n, 4 + x // 2, ((2 * x + h) % 4) * P:((2 * x + h) % 4 + 1) * P],
                                  pr[:, u % 2, x, a:a + n])
                mm.then_inc(pt_t, 1)

            def weigh_values(u):
                pe.wait_ge(pt_a, u + 1)
                pe.wait_ge(pt_d, u + 1)
                if u:
                    pe.wait_ge(o_norm, u)
                if u < A_UNITS - 1:
                    for x in range(4):
                        g, b = x // 2, 2 * (u % 4) + x % 2
                        for h in range(2):
                            if b + h:
                                mm = pe.matmul(ps[:, 6, x * HD:(x + 1) * HD], pt[:, 2 * x + h, :],
                                               vr[:, b - 1 + h, g * HD:(g + 1) * HD],
                                               start=(h == 0 or b == 0), stop=(h == 1))
                else:
                    pe.wait_ge(late_in, 16 * 3)
                    for b in range(NB_DEC):
                        for g in range(KVH):
                            x, part = 2 * g + b // 4, slice(32 * (b % 4), 32 * (b % 4) + 32)
                            out = ps[part, 6, x * HD:(x + 1) * HD]
                            pe.matmul(out, pt[:, 2 * x, part], vcache[:, b, g * HD:(g + 1) * HD], start=True, stop=False)
                            mm = pe.matmul(out, pt[0:T_DEC, 2 * x + 1, part], vnew[:, b, g * HD:(g + 1) * HD],
                                           start=False, stop=True)
                mm.then_inc(pv, 1)

            def turn_outputs(u):
                pe.wait_ge(o_norm, u + 1)
                if u:
                    pe.wait_ge(o_lo, 2 * u)
                for half in range(2):
                    mm = turn(ps[:, 7, half * P:(half + 1) * P], orow[:, half, :, :].rearrange("p g d -> p (g d)"))
                mm.then_inc(o_t, 1)

            def filler_group(i):
                n, c = filler(i)
                need(n)
                full_group(g_in(n, c), n, c)

            filler_group(0)
            for s in range(A_STEPS):
                if s < A_UNITS:
                    score_products(s)
                if 0 <= s - 2 < A_UNITS:
                    weigh_values(s - 2)
                if 0 <= s - 3 < A_UNITS:
                    turn_outputs(s - 3)
                if s + 1 < FILL:
                    filler_group(s + 1)
                if 0 <= s - 1 < A_UNITS:
                    turn_probs(s - 1)

            def gate_groups(j):
                for x in range(2):
                    need(U_D + 3 * j + x)
                    for c in range(NC_):
                        full_group(g_gate(j, x, c), U_D + 3 * j + x, c)

            pe.wait_ge(s_free, A_UNITS)
            gate_groups(0)

            pe.wait_ge(pooled, PT_)
            pe.wait_ge(o_lo, 2 * A_UNITS)
            for t in range(PT_):
                turn(ps[0:PSTATE, 6, t * P:(t + 1) * P], tails[:, t, 0:PSTATE])
            for t in range(PT_):
                mm = turn(ps[0:SROWS, 7, t * P:(t + 1) * P], tails[:, t, PSTATE:])
            mm.then_inc(st_o, 1)
            for t in range(PT_):
                for c in range(NC_):
                    g = G_GRP + NC_ * t + c
                    bank_free(g)
                    c0, w = CH[c]
                    np_ = min(w, SEQ - c0)
                    mm = pe.matmul(ps[:, bank_of(g), 0:np_], wgrp[:, t, :], upp[:, t, c0:c0 + np_],
                                   start=True, stop=True)
                    if w > np_:
                        mm = pe.matmul(ps[:, bank_of(g), np_:w], wgrp[:, t, :], ups[:, t, :, PSTATE:], start=True, stop=True)
                    mm.then_inc(done, 1)

            for j in range(KD):
                n = U_D + 3 * j
                if j:
                    gate_groups(j)
                need(n + 2)
                for c, x in mix_order(j):
                    if (j, c, x) == (0, 0, 1):
                        pe.wait_ge(freed["D"], FREED[G_GRP + NC_ * PT_ - 1][1])
                    g = g_mix(j, c, x)
                    bank_free(g)
                    products(ps[:, bank_of(g), 0:CH[c][1]],
                             [(wtile(n + 2, 4 * x + k), rows((qo, zz)[x], k, c)) for k in range(4)], True)

            def feature_sum(s, src, w):
                if s:
                    pe.wait_ge(n_sd, s)
                pe.matmul(ps[:, 4, 0:w], ones[:, :], src[:, 0:w], start=True, stop=True).then_inc(n_sum, 1)

            def x_again(c, m):
                c0, w = CH[c]
                if 1 <= m <= 4:
                    for k in (2 * m - 2, 2 * m - 1):
                        if k == 0:
                            pe.wait_ge(xr_in, 16 * min(3 * c + 3, RT))
                        if KD * c + k >= 2:
                            pe.wait_ge(n_h, KD * c + k - 1)
                        for r in range((w + P - 1) // P):
                            n = min(P, w - r * P)
                            src = xre[:, k, c0 + r * P:c0 + r * P + P] if n == P else xre_s[:, k, :]
                            mm = turn(ps[:, 5 + k % 2, r * P:r * P + n], src, n)
                        mm.then_inc(xr_t, 1)

            def norm_sums(c, m):
                if m == 0:
                    pe.wait_ge(e_add, 7 * (c + 1))
                    feature_sum(2 * c, ssa, CH[c][1])
                elif m == 5:
                    pe.wait_ge(n_add, 7 * (c + 1))
                    feature_sum(2 * c + 1, ssb, CH[c][1])

            def up_group(blk, j, c, n):
                g = g_up(blk, j, c)
                if isinstance(blk, int):
                    bank_free(g)
                    h, l = slot(n)
                else:
                    q1 = before_in_bank(g_up(1, j, c))
                    assert FREED[q1][0] == FREED[before_in_bank(g_up(2, j, c))][0]
                    pe.wait_ge(freed[FREED[q1][0]], per_block(lambda b: FREED[before_in_bank(g_up(b, j, c))][1], blk))
                    h, l = wr[:, n % 2, 0, :], wr[:, n % 2, 1, :]
                products(ps[:, bank_up(blk, j, c), 0:CH[c][1]],
                         [((h[:, k * P:(k + 1) * P], l[:, k * P:(k + 1) * P]), rows(xn, k, c)) for k in range(KD)], True)

            def down_group(blk, m, c, n):
                g = g_down(blk, m, c)
                col, w = (ycs(c), YCH[c][1]) if is_block(blk, LAST) else (cs(c), CH[c][1])
                if isinstance(blk, int):
                    bank_free(g)
                    h, l = slot(n)
                else:
                    q1 = before_in_bank(g_down(1, m, c))
                    pe.wait_ge(freed[FREED[q1][0]], per_block(lambda b: FREED[before_in_bank(g_down(b, m, c))][1], blk))
                    h, l = wr[:, n % 2, 0, :], wr[:, n % 2, 1, :]
                a = [slice(k * 2 * P + (m % 2) * P, k * 2 * P + (m % 2) * P + P) for k in range(FB)]
                products(ps[:, bank_down(blk, m, c), 0:w],
                         [((h[:, a[k]], l[:, a[k]]), (ff[:, 0, k, col], ff[:, 1, k, col])) for k in range(FB)], True)

            for st in range(NC_ + 1):
                for m in range(KD):
                    if st < NC_:
                        if m == 0:
                            pe.wait_ge(m_lo, 2 * st + 2)
                        if st == 0:
                            need(U_E + m)
                        full_group(G_E + KD * st + m, U_E + m, st)
                    else:
                        j, c = STAGE3[m]
                        if c == 0:
                            need(U_M + j)
                        if j == 0:
                            pe.wait_ge(n2_lo, KD * (c + 1))
                        up_group(0, j, c, U_M + j)
                    if st:
                        x_again(st - 1, m)
                        norm_sums(st - 1, m)
            need(U_M + FB)
            for m, c in EARLY:
                if m == 0:
                    pe.wait_ge(f_lo, e_up(0, FB - 1, c) + 1)
                down_group(0, m, c, U_M + FB)
            pe.wait_ge(n2_lo, KD * NC_)
            for j in range(FB):
                up_group(0, j, 2, U_M + j)
            for m, c in DOWN0:
                if m % 2 == 0 and c == 0:
                    need(U_M + FB + m // 2)
                if (m, c) == (0, 2):
                    pe.wait_ge(f_lo, e_up(0, FB - 1, c) + 1)
                down_group(0, m, c, U_M + FB + m // 2)

            def mlp_block(blk):
                for j, c in MAIN:
                    if c == 0:
                        pe.wait_ge(w_lo, blk * 8 + (U_M + j + 1))
                    up_group(blk, j, c, U_M + j)
                for m, c in DOWN:
                    if m % 2 == 0 and c == 0:
                        pe.wait_ge(w_lo, blk * 8 + (U_M + FB + m // 2 + 1))
                    if m == 0:
                        pe.wait_ge(f_lo, e_up(blk, FB - 1, c) + 1)
                    down_group(blk, m, c, U_M + FB + m // 2)

            with pe.Fori(1, LAST) as blk:
                mlp_block(blk)
            for j, c in MAIN:
                n = U_M + 8 * LAST + j
                if c == 0:
                    need(n)
                up_group(LAST, j, c, n)

            def y_part(c, m):
                if m == 1:
                    pe.wait_ge(e_add, 7 * (NC_ + c + 1))
                    if c == 2:
                        pe.wait_ge(y_r[0], 3)
                    feature_sum(2 * NC_ + c, ssy, YCH[c][1])
                tiles = Y_AT.get((c + 1, m), [])
                for half in range(2):
                    if half == 0 and tiles:
                        pe.wait_ge(n_sd, 2 * NC_ + c + 1)
                        if tiles[0] >= 2:
                            pe.wait_ge(y_r[0], tiles[-1] - 1)
                            pe.wait_ge(y_r[1], tiles[-1] - 1)
                    for k in range(4 * half, 4 * half + 4):
                        for r in tiles:
                            if r == tiles[0]:
                                q = KD // 2 * y_chunk(r) + k // 2 + 1
                                if k % 2:
                                    pe.wait_ge(y_hp, q)
                                else:
                                    pe.wait_ge(y_h, q)
                            n = min(P, ROWS - r * P)
                            mm = turn(ps[0:n, 4 + 2 * (r % 2) + half, (k % 4) * P:(k % 4 + 1) * P],
                                      hh[:, k, r * P:r * P + n])
                            if k % 4 == 3:
                                mm.then_inc(y_p, 1)

            for st in range(NC_ + 1):
                for m in range(KD):
                    if st < NC_:
                        n = U_LASTD + m // 2
                        if st == 0 and m % 2 == 0:
                            need(n)
                        if m == 0:
                            pe.wait_ge(f_lo, e_up(LAST, FB - 1, min(st + 1, 2)) + 1)
                        down_group(LAST, m, st, n)
                    if st:
                        y_part(st - 1, m)


def bucket_onehot():
    half = BUCKETS // 2
    out = np.zeros((BUCKETS, WIN), np.float32)
    for n in range(WIN):
        d = WIN - 1 - n
        b = d if d < half else min(BUCKETS - 1, half + int(math.log(d / half) / math.log(MAXD / half) * (BUCKETS - half)))
        out[b, n] = 1.0
    return out


def query_perm():
    out = np.zeros((32, P), np.float32)
    for p in range(P):
        i, t = (p // T_DEC) % GRP, p % T_DEC
        out[i * T_DEC + T_DEC - 1 - t, p] = 1.0
    return out


def inv_count():
    return np.array([[1.0 / min(n + 1, 2 ** (t + 1)) for t in range(PT_) for n in range(16)]], np.float32)


def vector_rows(x):
    b = x["b_in"][0]
    q = b[:AW].reshape(KVH, GRP, HD).transpose(1, 0, 2).reshape(-1)
    parts = [q, b[AW:], x["norm_pre_mix"][0], x["norm_post_mix"][0], x["norm_pre_mlp"][0], x["norm_post_mlp"][0],
             x["pool_scale"][0]]
    return np.concatenate(parts).reshape(-1, P)


def sink_rows(x):
    return np.repeat(x["attn_sinks"][0].reshape(KVH, GRP).T, T_DEC, axis=0)


def weight_units(x):
    def by_tile(w):
        k, n = w.shape
        return w.reshape(k // P, P, n // P, P).transpose(2, 1, 0, 3)

    w = x["w_in"][0]
    q = by_tile(w[:, :AW].reshape(D, KVH, GRP, HD).transpose(0, 2, 1, 3).reshape(D, AW))
    k, v, up = by_tile(w[:, COL_K:COL_V]), by_tile(w[:, COL_V:COL_UP]), by_tile(w[:, COL_UP:COL_GA])
    ga, gp = by_tile(w[:, COL_GA:COL_GP]), by_tile(w[:, COL_GP:])
    au = x["w_attn_up"][0].reshape(KVH, GRP, HD, D).transpose(1, 0, 2, 3).reshape(AW, D)
    both = np.concatenate([by_tile(au), by_tile(x["w_pool_up"][0])], axis=2)
    mid = np.stack([ga, gp, both], axis=1).reshape(-1, P, D)
    mlp_up = by_tile(x["w_mlp_up"][0]).reshape(NFB, FB, P, D)
    mlp_down = x["w_mlp_down"][0].reshape(NFB, FB, P, 4, 2 * P).transpose(0, 3, 2, 1, 4).reshape(NFB, 4, P, D)
    mlp = np.concatenate([mlp_up, mlp_down], axis=1).reshape(-1, P, D)
    parts = [k, v, q, up, mid, by_tile(x["w_out"][0]), mlp]
    return np.concatenate([a.reshape(-1, P, D) for a in parts])


_INS = ["x_prompt", "x_sample", "cache_k_win", "cache_v_win", "state_pool", "norm_pre_mix", "attn_sinks",
        "rel_bias_table", "w_pool_grp"]
_OUTS = [("y_prompt", (1, SEQ, D)), ("y_sample", (NB_DEC, T_DEC, D)),
         ("k_win_prompt", (1, 1, WIN, KVH, HD)), ("v_win_prompt", (1, 1, WIN, KVH, HD)),
         ("pool_state_prompt", (1, 1, PSTATE, PW)),
         ("k_win_sample", (1, NB_DEC, WIN, KVH, HD)), ("v_win_sample", (1, NB_DEC, WIN, KVH, HD)),
         ("pool_state_sample", (1, NB_DEC, PSTATE, PW))]


def kernel(**inputs):
    import numpy as _np
    import concourse.bacc as _bacc
    from concourse import mybir as _mybir
    from concourse.bass_utils import run_bass_kernel_spmd as _run

    nc = _bacc.Bacc("TRN2", target_bir_lowering=False, num_devices=1)
    arrays, ins, outs = {}, {}, {}
    x = {name: _np.ascontiguousarray(a) for name, a in inputs.items()}
    given = {name: x[name] for name in _INS}
    given.update(weights=weight_units(x), vectors=vector_rows(x), sink_rows=_np.ascontiguousarray(sink_rows(x)),
                 bucket_onehot=bucket_onehot(), query_perm=query_perm(), inv_count=inv_count())
    for name, a in given.items():
        arrays[f"in_{name}"] = a
        ins[name] = nc.dram_tensor(f"in_{name}", a.shape, _mybir.dt.from_np(a.dtype), kind="ExternalInput").ap()
    for name, shape in _OUTS:
        outs[name] = nc.dram_tensor(f"out_{name}", shape, _mybir.dt.float32, kind="ExternalOutput").ap()
    build(nc, ins, outs)
    r = _run(nc, [arrays], core_ids=[0])
    return tuple(r.results[0][f"out_{name}"] for name, _ in _OUTS)
```
